# Optimizing a Trainium2 kernel written in Bass

```python
import jax, jax.numpy as jnp
from jax import lax
import numpy as np

D_MODEL = 1024
BATCH = 1
SEQ = 1024
DEPTH = 2

CHUNK = 64
N_MIXERS = 2
POOL_WINDOWS = (2, 4, 8, 16)
N_POOL_GROUPS = len(POOL_WINDOWS)
POOL_GROUP = D_MODEL // N_POOL_GROUPS
N_HEADS = 8
HEAD_DIM = D_MODEL // N_HEADS
CONV_WIDTH = 4
D_FF = 4 * D_MODEL
RMS_EPS = 1e-6
PROJ_WIDTH = 4 * D_MODEL + 2 * N_HEADS
N_POOL_LAYERS = (DEPTH + 1) // 2
N_MLSTM_LAYERS = DEPTH // 2

kernel_name = "hybrid_pool_mlstm_sandwich_trunk"

def rmsnorm(x, g):
    xf = x.astype(jnp.float32)
    y = xf * lax.rsqrt(jnp.mean(xf * xf, axis=-1, keepdims=True) + RMS_EPS)
    return (y * g.astype(jnp.float32)).astype(x.dtype)

def pool_mixer(h, w_grp, b, scale):
    B, S, D = h.shape
    hf = h.astype(jnp.float32)
    cs0 = jnp.concatenate([jnp.zeros((B, 1, D), jnp.float32), jnp.cumsum(hf, axis=1)], axis=1)
    t = jnp.arange(S, dtype=jnp.float32)
    parts = []
    for g, w in enumerate(POOL_WINDOWS):
        c = cs0[:, :, g * POOL_GROUP:(g + 1) * POOL_GROUP]
        upper = c[:, 1:]
        lower = jnp.pad(c[:, :S - w + 1], ((0, 0), (w - 1, 0), (0, 0)))
        count = jnp.minimum(t + 1.0, float(w))
        parts.append((upper - lower) / count[None, :, None])
    pooled = jnp.concatenate(parts, axis=-1) - hf
    pooled = pooled.reshape(B, S, N_POOL_GROUPS, POOL_GROUP)
    y = jnp.einsum('bsgc,gcd->bsgd', pooled, w_grp.astype(jnp.float32)).reshape(B, S, D)
    y = (y + b.astype(jnp.float32)) * scale.astype(jnp.float32)
    return y.astype(h.dtype)

def causal_depthwise_conv(u, w, b):
    S = u.shape[1]
    up = jnp.pad(u, ((0, 0), (CONV_WIDTH - 1, 0), (0, 0)))
    out = b.astype(jnp.float32)
    for j in range(CONV_WIDTH):
        out = out + w[j].astype(jnp.float32) * up[:, j:j + S]
    return out

def mlstm_chunk_step(carry, inp):
    C, n, m = carry
    q, k, v, ig, lf = inp
    L = q.shape[2]
    causal = jnp.tril(jnp.ones((L, L), dtype=bool))
    b = jnp.cumsum(lf, axis=-1)
    log_d = b[..., :, None] - b[..., None, :] + ig[..., None, :]
    log_d = jnp.where(causal, log_d, -jnp.inf)
    m_inter = b + m[..., None]
    m_out = jnp.maximum(jnp.max(log_d, axis=-1), m_inter)
    s = jnp.einsum('bhtd,bhsd->bhts', q, k) * jnp.exp(log_d - m_out[..., None])
    inter = jnp.exp(m_inter - m_out)
    num = jnp.einsum('bhts,bhsd->bhtd', s, v) + inter[..., None] * jnp.einsum('bhtk,bhkv->bhtv', q, C)
    den = jnp.sum(s, axis=-1) + inter * jnp.einsum('bhtk,bhk->bht', q, n)
    h = num / jnp.maximum(jnp.abs(den), jnp.exp(-m_out))[..., None]
    g = b[..., -1]
    a = g[..., None] - b + ig
    m_new = jnp.maximum(g + m, jnp.max(a, axis=-1))
    decay = jnp.exp(g + m - m_new)
    wts = jnp.exp(a - m_new[..., None])
    C_new = decay[..., None, None] * C + jnp.einsum('bhs,bhsk,bhsv->bhkv', wts, k, v)
    n_new = decay[..., None] * n + jnp.einsum('bhs,bhsk->bhk', wts, k)
    return (C_new, n_new, m_new), h

def mlstm_mixer(h, w_in, conv_w, conv_b, i_bias, f_bias, head_norm_w, w_out):
    B, S, D = h.shape
    NC = S // CHUNK
    proj = jnp.einsum('bsd,de->bse', h, w_in).astype(jnp.float32)
    qk = proj[..., :2 * D]
    v = proj[..., 2 * D:3 * D]
    o_pre = proj[..., 3 * D:4 * D]
    i_pre = proj[..., 4 * D:4 * D + N_HEADS]
    f_pre = proj[..., 4 * D + N_HEADS:]
    qk = jax.nn.silu(causal_depthwise_conv(qk, conv_w, conv_b))
    q = qk[..., :D]
    k = qk[..., D:] * (HEAD_DIM ** -0.5)
    ig = i_pre + i_bias.astype(jnp.float32)
    lf = jax.nn.log_sigmoid(f_pre + f_bias.astype(jnp.float32))

    def to_chunks(a):
        return a.reshape(B, NC, CHUNK, N_HEADS, HEAD_DIM).transpose(1, 0, 3, 2, 4)

    def gate_chunks(a):
        return a.reshape(B, NC, CHUNK, N_HEADS).transpose(1, 0, 3, 2)

    init = (jnp.zeros((B, N_HEADS, HEAD_DIM, HEAD_DIM), jnp.float32),
            jnp.zeros((B, N_HEADS, HEAD_DIM), jnp.float32),
            jnp.zeros((B, N_HEADS), jnp.float32))
    _, hc = lax.scan(mlstm_chunk_step, init,
                     (to_chunks(q), to_chunks(k), to_chunks(v), gate_chunks(ig), gate_chunks(lf)))
    hs = hc.transpose(1, 0, 3, 2, 4).reshape(B, S, N_HEADS, HEAD_DIM)
    hs = hs * lax.rsqrt(jnp.mean(hs * hs, axis=-1, keepdims=True) + RMS_EPS)
    hs = hs.reshape(B, S, D) * head_norm_w.astype(jnp.float32)
    gated = jax.nn.sigmoid(o_pre) * hs
    return jnp.einsum('bsd,de->bse', gated.astype(h.dtype), w_out)

def sq_relu_mlp(h, w1, w2):
    a = jax.nn.relu(jnp.einsum('bsd,df->bsf', h, w1))
    return jnp.einsum('bsf,fd->bsd', a * a, w2)

def setup_inputs(seed: int = 0) -> dict:
    key = jax.random.key(seed)
    ks = jax.random.split(key, 20)
    nrm = jax.random.normal
    f32 = jnp.float32
    x = nrm(ks[0], (BATCH, SEQ, D_MODEL), f32)
    mix_pre_g = 1.0 + 0.02 * nrm(ks[1], (DEPTH, D_MODEL), f32)
    mix_post_g = 1.0 + 0.02 * nrm(ks[2], (DEPTH, D_MODEL), f32)
    ffn_pre_g = 1.0 + 0.02 * nrm(ks[3], (DEPTH, D_MODEL), f32)
    ffn_post_g = 1.0 + 0.02 * nrm(ks[4], (DEPTH, D_MODEL), f32)
    pool_w = nrm(ks[5], (N_POOL_LAYERS, N_POOL_GROUPS, POOL_GROUP, POOL_GROUP), f32) * POOL_GROUP ** -0.5
    pool_b = 0.02 * nrm(ks[6], (N_POOL_LAYERS, D_MODEL), f32)
    pool_scale = 1.0 + 0.1 * nrm(ks[7], (N_POOL_LAYERS, D_MODEL), f32)
    mlstm_w_in = nrm(ks[8], (N_MLSTM_LAYERS, D_MODEL, PROJ_WIDTH), f32) * D_MODEL ** -0.5
    mlstm_conv_w = nrm(ks[9], (N_MLSTM_LAYERS, CONV_WIDTH, 2 * D_MODEL), f32) * CONV_WIDTH ** -0.5
    mlstm_conv_b = 0.02 * nrm(ks[10], (N_MLSTM_LAYERS, 2 * D_MODEL), f32)
    mlstm_i_bias = 0.1 * nrm(ks[11], (N_MLSTM_LAYERS, N_HEADS), f32)
    mlstm_f_bias = (jnp.linspace(3.0, 6.0, N_HEADS, dtype=f32)[None, :]
                    + 0.1 * nrm(ks[12], (N_MLSTM_LAYERS, N_HEADS), f32))
    mlstm_head_norm_w = 1.0 + 0.02 * nrm(ks[13], (N_MLSTM_LAYERS, D_MODEL), f32)
    mlstm_w_out = nrm(ks[14], (N_MLSTM_LAYERS, D_MODEL, D_MODEL), f32) * D_MODEL ** -0.5
    mlp_w1 = nrm(ks[15], (DEPTH, D_MODEL, D_FF), f32) * D_MODEL ** -0.5
    mlp_w2 = nrm(ks[16], (DEPTH, D_FF, D_MODEL), f32) * D_FF ** -0.5
    return {"x": x, "mix_pre_g": mix_pre_g, "mix_post_g": mix_post_g,
            "ffn_pre_g": ffn_pre_g, "ffn_post_g": ffn_post_g,
            "pool_w": pool_w, "pool_b": pool_b, "pool_scale": pool_scale,
            "mlstm_w_in": mlstm_w_in, "mlstm_conv_w": mlstm_conv_w, "mlstm_conv_b": mlstm_conv_b,
            "mlstm_i_bias": mlstm_i_bias, "mlstm_f_bias": mlstm_f_bias,
            "mlstm_head_norm_w": mlstm_head_norm_w, "mlstm_w_out": mlstm_w_out,
            "mlp_w1": mlp_w1, "mlp_w2": mlp_w2}

def reference(x, mix_pre_g, mix_post_g, ffn_pre_g, ffn_post_g,
              pool_w, pool_b, pool_scale,
              mlstm_w_in, mlstm_conv_w, mlstm_conv_b, mlstm_i_bias, mlstm_f_bias,
              mlstm_head_norm_w, mlstm_w_out, mlp_w1, mlp_w2):
    for i in range(DEPTH):
        j = i // N_MIXERS
        hn = rmsnorm(x, mix_pre_g[i])
        if i % N_MIXERS == 0:
            y = pool_mixer(hn, pool_w[j], pool_b[j], pool_scale[j])
        else:
            y = mlstm_mixer(hn, mlstm_w_in[j], mlstm_conv_w[j], mlstm_conv_b[j],
                            mlstm_i_bias[j], mlstm_f_bias[j], mlstm_head_norm_w[j], mlstm_w_out[j])
        x = x + rmsnorm(y, mix_post_g[i])
        hn = rmsnorm(x, ffn_pre_g[i])
        y = sq_relu_mlp(hn, mlp_w1[i], mlp_w2[i])
        x = x + rmsnorm(y, ffn_post_g[i])
    return x


_drawn_inputs = setup_inputs


def setup_inputs(seed=0):
    import zlib

    import numpy as np

    out = dict(_drawn_inputs(seed))
    spreads = {}
    factors = {'mix_post_g': 2.89,
     'ffn_pre_g': 9.132,
     'ffn_post_g': 8.855,
     'mlstm_conv_b': 8.0,
     'mlstm_i_bias': 64.0,
     'mlstm_head_norm_w': 26.815}
    for name, (base, spread) in spreads.items():
        noise = np.random.default_rng([zlib.crc32(name.encode()), seed]).standard_normal(out[name].shape)
        drawn = base * np.exp(spread * noise) if base else spread * noise
        out[name] = __import__('jax').numpy.asarray(drawn.astype(out[name].dtype))
    for name, factor in factors.items():
        out[name] = (out[name] * factor).astype(out[name].dtype)
    return out
```

```python
from contextlib import ExitStack

import numpy as np

import concourse.bass as bass
from concourse import mybir

ALU = mybir.AluOpType
ACT = mybir.ActivationFunctionType
F32 = mybir.dt.float32
F32R = mybir.dt.float32r
RADD = bass.bass_isa.ReduceOp.add

P = 128
D = 1024
SEQ = 1024
HALVES = 2
T = SEQ // HALVES
KT = D // P
D_FF = 4 * D
HEADS = 8
HEAD_DIM = D // HEADS
TAPS = 4
LC = 128
CPH = T // LC
WINDOWS = (2, 4, 8, 16)
GROUP = D // len(WINDOWS)
HALO = 16
EPS = 1e-6
KSCALE = HEAD_DIM ** -0.5
NEG = -1e30

BLK = 8 * P
FT = 4
W1_BLOCKS = FT
W2_BLOCKS = KT // 2
CHUNK_BLOCKS = W1_BLOCKS + W2_BLOCKS
CHUNKS = D_FF // (FT * P)
POOL_BLOCKS = 2
HEAD_BLOCKS = 4
GATE_ROW_F = 32
D_POOL = 0
D_MLP = (POOL_BLOCKS, POOL_BLOCKS + CHUNKS * CHUNK_BLOCKS + 1 + HEADS * HEAD_BLOCKS + 2 * W2_BLOCKS)
D_GATE = D_MLP[0] + CHUNKS * CHUNK_BLOCKS
D_HEAD = D_GATE + 1
D_OUT = D_HEAD + HEADS * HEAD_BLOCKS
DRAM_BLOCKS = D_MLP[1] + CHUNKS * CHUNK_BLOCKS

RAW = 2
SPLIT = 2
BANKS = 4
STEPS = HALVES * HEADS

V_MIX_PRE, V_MIX_POST, V_FFN_PRE, V_FFN_POST = 0, 16, 32, 48
V_POOL_B, V_POOL_S = 64, 72
V_CONV_W, V_CONV_B = 80, 144
V_HEAD_NORM, V_GATE_B = 160, 168
VECS = 169
C_IDENT, C_MASK, C_INV = 0, P, P + T
CONSTS = P + T + len(WINDOWS) * HALO

MLP_INTERLUDES = {
    (0, 0): {0: "norm", 1: None, 2: "pool", 3: "norm", 5: "norm"},
    (0, 1): {0: "norm", 2: "norm"},
    (1, 0): {0: "norm", 2: "norm"},
    (1, 1): {0: "norm"},
}
LSTM_NORM_STEPS = (2, 5, 11, 14)
WINDOW_CHUNKS = (1, 2)


def segments(layer, half):
    marks = MLP_INTERLUDES[layer, half]
    last = {CHUNKS - 2} if (layer, half) == (1, 1) else set()
    cuts = sorted({0, CHUNKS - 1, *marks, *last})
    out, at = [], 0
    for c in cuts:
        out.append((at, c + 1, marks.get(c)))
        at = c + 1
    return out


def heads_out(j):
    return j // FT - 1 if j > FT and j % FT == 1 else None


def plan():
    p = {"block": {}, "dram": [], "group": {}, "evac": [], "block_end": []}
    evacs = {"dve": 0, "act": 0}

    def block(key, dram):
        p["block"][key] = len(p["dram"])
        p["dram"].append(dram)

    def group(key, engine):
        p["group"][key] = len(p["evac"])
        evacs[engine] += 1
        p["evac"].append((engine, evacs[engine]))

    def block_ends():
        p["block_end"].append(len(p["evac"]))

    def pool(half):
        for b in range(POOL_BLOCKS):
            block(("pool", half, b), D_POOL + b)
            for d in range(4):
                group(("pool", half, 4 * b + d), "dve" if half else "act")
            block_ends()

    def mlp(layer, half):
        for c in range(CHUNKS):
            for f in range(W1_BLOCKS):
                block(("w1", layer, half, c, f), D_MLP[layer] + c * CHUNK_BLOCKS + f)
                group(("w1", layer, half, c, f), "act")
                block_ends()
            for b in range(W2_BLOCKS):
                block(("w2", layer, half, c, b), D_MLP[layer] + c * CHUNK_BLOCKS + W1_BLOCKS + b)
                for d in range(2):
                    group(("w2", layer, half, c, 2 * b + d), "dve")
                block_ends()
            if MLP_INTERLUDES[layer, half].get(c) == "pool":
                pool(1)

    def project_out(g):
        for b in range(W2_BLOCKS):
            block(("out", g, b), D_OUT + (g % 2) * W2_BLOCKS + b)
            for d in range(2):
                group(("out", g, 2 * b + d), "dve")
            block_ends()

    pool(0)
    mlp(0, 0)
    mlp(0, 1)
    for j in range(STEPS):
        if heads_out(j) is not None:
            project_out(heads_out(j))
        if j % HEADS == 0:
            block(("gate", j // HEADS), D_GATE)
            group(("gate", j // HEADS), "dve")
            block_ends()
        for t in range(HEAD_BLOCKS):
            block(("head", j, t), D_HEAD + (j % HEADS) * HEAD_BLOCKS + t)
            group(("head", j, t), "act")
            block_ends()
    project_out(STEPS // FT - 1)
    mlp(1, 0)
    mlp(1, 1)
    return p


class OwnSteps:

    def __init__(self, engine, sem):
        self.engine, self.sem, self.n, self.loop = engine, sem, 0, 0

    def finish(self, ins):
        self.n += 1
        ins.then_inc(self.sem, 1)
        self.engine.wait_ge(self.sem, self.n + self.loop)

    def repeat(self, i, per):
        self.loop = i * per
        self.start, self.per = self.n, per

    def repeated(self, times):
        assert self.n - self.start == self.per, (self.n - self.start, self.per)
        self.n, self.loop = self.start + self.per * times, 0


def build(nc, x_in, weights, vecs_in, consts_in, out):
    plan_ = plan()
    BLOCK, DRAM, GROUPS, EVAC, BLOCK_END = (
        plan_["block"], plan_["dram"], plan_["group"], plan_["evac"], plan_["block_end"])
    NB = len(DRAM)

    with ExitStack() as ctx:
        def sb(name, shape, dt=F32):
            return ctx.enter_context(nc.sbuf_tensor(name, shape, dt))

        def psum(name, shape):
            return ctx.enter_context(nc.psum_tensor(name, shape, F32))

        def sem(name):
            return ctx.enter_context(nc.semaphore(name))

        hn_hi = [sb(f"hn_hi{h}", [P, KT, T], F32R) for h in range(HALVES)]
        hn_lo = [sb(f"hn_lo{h}", [P, KT, T], F32R) for h in range(HALVES)]
        y = [sb(f"y{h}", [P, KT, T]) for h in range(HALVES)]
        hid_hi = sb("hid_hi", [P, FT, T], F32R)
        hid_lo = sb("hid_lo", [P, FT, T], F32R)
        raw = sb("raw", [P, RAW, BLK])
        w_hi = sb("w_hi", [P, SPLIT, BLK], F32R)
        w_lo = sb("w_lo", [P, SPLIT, BLK], F32R)
        vecs = sb("vecs", [P, VECS])
        consts = sb("consts", [P, CONSTS])
        ident = consts[:, C_IDENT:C_IDENT + P]
        mask = consts[:, C_MASK:C_MASK + T]
        eps = sb("eps", [P, 1])
        sq = sb("sq", [P, T])
        acc = sb("acc", [P, T])
        tot = sb("tot", [P, T])
        rstd = sb("rstd", [P, T])
        xold = sb("xold", [P, 2, T])
        step_t = sb("step_t", [P, T])
        relu_sq = sb("relu_sq", [P, T])
        ones = sb("ones", [P, P])
        pool_bs = sb("pool_bs", [P, KT])
        craw = sb("craw", [P, 2, HALO + T])
        taps = sb("taps", [P, 2 * HEADS, HALO])
        win = sb("win", [P, 2, HALO + T])
        qT = sb("qT", [P, 2, T])
        kT = sb("kT", [P, T])
        vT = sb("vT", [P, T])
        oT = sb("oT", [P, 2, T])
        mx_b = sb("mx_b", [P, 2, T])
        inter_b = sb("inter_b", [P, 2, T])
        qs = sb("qs", [P, T])
        kw = sb("kw", [P, T])
        v_tok = sb("v_tok", [P, CPH, HEAD_DIM + 1])
        prob = sb("prob", [P, T])
        hnorm = sb("hnorm", [P, T])
        state = sb("state", [P, HEADS, HEAD_DIM + 1])
        mid = sb("mid", [P, CPH - 1, HEAD_DIM + 1])
        rows = sb("rows", [P, T])
        cols = sb("cols", [P, 2, CPH, P])
        small = sb("small", [P, 8, CPH])
        zrow = sb("zrow", [HEADS, LC])
        m_run = sb("m_run", [HEADS, STEPS])

        relu = [kw, prob]
        parts = [sq, acc]
        squares = [qs, vT, kT, oT[:, 0, :]]

        bank = [psum(f"bank{i}", [P, T]) for i in range(BANKS)]
        core = [psum(f"core{i}", [P, T]) for i in range(4)]

        x_scratch = nc.dram_tensor("x_scratch", [HALVES, KT, P, T], F32).ap()
        row_scratch = nc.dram_tensor("row_scratch", [HALVES, 2, HEADS, T], F32).ap()

        vecs_in_s = sem("vectors_landed")
        x_in_s = [sem(f"x_in_landed{i}") for i in range(KT // 2 + 1)]
        bs_ready = sem("pool_bias_ready")
        sq_ready = sem("square_ready")
        sq_summed = sem("square_summed")
        hn0_part = sem("hn0_part_ready")
        hn0_hi = sem("hn0_high_ready")
        hn0_tiles = sem("hn0_tiles_ready")
        hidhi_ready = sem("hidden_high_ready")
        consts_set = sem("consts_set")
        raw_landed = [sem(f"raw_landed{i}") for i in range(RAW)]
        hi_ready = sem("w_hi_ready")
        lo_ready = sem("w_lo_ready")
        group_done = sem("group_done")
        evac_s = {"dve": sem("evac_dve"), "act": sem("evac_act")}
        hid_ready = sem("hidden_ready")
        hn_ready = sem("hn_ready")
        pooled_ready = sem("pooled_ready")
        xn_ready = sem("normed_tile_ready")
        xn_used = sem("normed_tile_used")
        acc_ready = sem("acc_ready")
        tot_ready = sem("total_ready")
        std_ready = sem("std_ready")
        rstd_ready = sem("rstd_ready")
        xold_landed = {w: [sem(f"xold_landed_{w}{i}") for i in range(2)] for w in ("act", "pool")}
        xold_used = sem("xold_used")
        xnew_ready = sem("xnew_ready")
        stored = {w: sem(f"x_stored_{w}") for w in ("act", "pool")}
        out_stored = {w: sem(f"out_stored_{w}") for w in ("act", "pool")}
        dve_own = sem("dve_own")
        act_own = sem("act_own")
        pool_own = sem("pool_own")
        craw_ready = sem("craw_ready")
        conv_ready = sem("conv_ready")
        qk_ready = sem("qk_ready")
        gate_z = sem("gate_z")
        gate_l = sem("gate_l")
        gate_args = sem("gate_args")
        gate_exp = sem("gate_exp")
        gate_rows = sem("gate_rows")
        gate_cols = sem("gate_cols")
        gate_cols_ready = sem("gate_cols_ready")
        rows_stored = sem("rows_stored")
        bcast_landed = [sem(f"bcast_landed{i}") for i in range(2)]
        mm_ready = sem("masked_max_ready")
        qs_ready = sem("qs_ready")
        turned = sem("core_turned")
        decays = sem("decay_matrix_ready")
        kw_ready = sem("kw_ready")
        vtok_ready = sem("v_tok_ready")
        prob_ready = sem("prob_ready")
        update_done = sem("state_updates_done")
        mid_ready = sem("mid_state_ready")
        state_ready = sem("state_ready")
        num_done = sem("numerators_done")
        ssq_ready = sem("head_ssq_ready")
        den_ready = sem("den_ready")
        hstd_ready = sem("head_std_ready")
        hnorm_ready = sem("hnorm_ready")
        hT_done = sem("head_turned_back")
        gated_ready = sem("gated_used")

        block = ctx.enter_context(nc.Block())

        CHAINS = [
            (("pool", 0), V_MIX_POST, V_FFN_PRE, "input"),
            (("pool", 1), V_MIX_POST, V_FFN_PRE, "input"),
            (("mlp0", 0), V_FFN_POST, V_MIX_PRE + 8, "scratch"),
            (("mlp0", 1), V_FFN_POST, V_MIX_PRE + 8, "scratch"),
            (("lstm", 0), V_MIX_POST + 8, V_FFN_PRE + 8, "scratch"),
            (("lstm", 1), V_MIX_POST + 8, V_FFN_PRE + 8, "scratch"),
            (("mlp1", 0), V_FFN_POST + 8, None, "scratch"),
            (("mlp1", 1), V_FFN_POST + 8, None, "scratch"),
        ]
        CHAIN = {key: n for n, (key, *_) in enumerate(CHAINS)}
        LAST_GROUP = {
            ("pool", 0): ("pool", 0, 7), ("pool", 1): ("pool", 1, 7),
            ("mlp0", 0): ("w2", 0, 0, CHUNKS - 1, 7), ("mlp0", 1): ("w2", 0, 1, CHUNKS - 1, 7),
            ("lstm", 0): ("out", 1, 7), ("lstm", 1): ("out", 3, 7),
            ("mlp1", 0): ("w2", 1, 0, CHUNKS - 1, 7), ("mlp1", 1): ("w2", 1, 1, CHUNKS - 1, 7),
        }
        NORM_FIRST = (0, 3)
        NORM_POST = (1, 4, 6, 8, 10, 12, 14, 15)
        NORM_PRE = (2, 5, 7, 9, 11, 13)
        FOREGROUND = (0, 1, 2, 15)
        EVACS = {"act": W1_BLOCKS, "dve": KT}

        def evacuated(eng, key, add=0):
            who, count = EVAC[GROUPS[key]]
            eng.wait_ge(evac_s[who], count + add)

        def hid_tile(layer, half, c):
            per = CHUNKS * FT
            if layer == "lstm":
                return 2 * per + FT * c
            return (2 * per + STEPS if layer else 0) + half * per + FT * c

        @block.sync
        def _(sp):
            def load(n, dram, loop_blocks=0):
                if n >= RAW:
                    sp.wait_ge(hi_ready, n - RAW + 1 + loop_blocks)
                    sp.wait_ge(lo_ready, n - RAW + 1 + loop_blocks)
                sp.dma_start(raw[:, n % RAW, :], dram).then_inc(raw_landed[n % RAW], 16)

            def loads(first, end):
                for n in range(first, end):
                    load(n, weights[DRAM[n]])

            def mlp(layer, half):
                for a, b, what in segments(layer, half):
                    n0 = BLOCK["w1", layer, half, a, 0]
                    if b - a > 1:
                        with sp.Fori(0, b - a) as i:
                            for k in range(CHUNK_BLOCKS):
                                at = i * CHUNK_BLOCKS + (DRAM[n0] + k)
                                load(n0 + k, weights[bass.ds(at, 1), :, :].rearrange("o p f -> (o p) f"),
                                     i * CHUNK_BLOCKS)
                    else:
                        loads(n0, n0 + CHUNK_BLOCKS)
                    if what == "pool":
                        loads(BLOCK["pool", 1, 0], BLOCK["pool", 1, 0] + POOL_BLOCKS)

            loads(0, POOL_BLOCKS)
            mlp(0, 0)
            mlp(0, 1)
            loads(BLOCK["gate", 0], BLOCK["w1", 1, 0, 0, 0])
            mlp(1, 0)
            mlp(1, 1)

        @block.tensor
        def _(pe):
            def split_ready(n, add=0):
                pe.wait_ge(hi_ready, n + 1 + add)
                pe.wait_ge(lo_ready, n + 1 + add)

            def bank_free(g, i=0):
                if g >= BANKS:
                    who, count = EVAC[g - BANKS]
                    pe.wait_ge(evac_s[who], count + i * EVACS[who])

            def sum_squares(n):
                for k in range(KT):
                    at = KT * FOREGROUND.index(n) + k
                    pe.wait_ge(sq_ready, at + 1)
                    nc.tensor.matmul(core[3][:, :], ones[:, :], squares[at % 4][:, :],
                                     start=(k == 0), stop=(k == KT - 1)).then_inc(sq_summed, 1)

            def three_passes(g, slot, cols_of, hi, lo, tiles, before=None):
                n, o = len(tiles), bank[g % BANKS][:, :]
                for k, t in enumerate(tiles):
                    if before:
                        before(k)
                    c = cols_of(k)
                    a, b = w_hi[:, slot, c:c + P], w_lo[:, slot, c:c + P]
                    nc.tensor.matmul(o, a, hi[:, t, :], start=(k == 0), stop=False)
                    nc.tensor.matmul(o, a, lo[:, t, :], start=False, stop=False)
                    last = nc.tensor.matmul(o, b, hi[:, t, :], start=False, stop=(k == n - 1))
                last.then_inc(group_done, 1)

            def pool(half):
                for b in range(POOL_BLOCKS):
                    n = BLOCK["pool", half, b]
                    split_ready(n)
                    for d in range(4):
                        g = GROUPS["pool", half, 4 * b + d]
                        bank_free(g)
                        w = 2 * b + d // 2
                        pe.wait_ge(pooled_ready, KT * half + 2 * w + 2)
                        three_passes(g, n % SPLIT, lambda k: (2 * (d // 2) + k) * GROUP + (d % 2) * P,
                                     hn_hi[half], hn_lo[half], [2 * w, 2 * w + 1])

            def second_product(n0, g0, tile0, i=0):
                split_ready(n0, i * CHUNK_BLOCKS)
                for ks in (range(FT - 1), [FT - 1]):
                    for d in range(2):
                        if ks[0] == 0:
                            bank_free(g0 + d, i)
                        o = bank[(g0 + d) % BANKS][:, :]
                        for k in ks:
                            if d == 0:
                                pe.wait_ge(hid_ready, tile0 + k + 1 + i * FT)
                            c = k * 2 * P + d * P
                            a, b = w_hi[:, n0 % SPLIT, c:c + P], w_lo[:, n0 % SPLIT, c:c + P]
                            nc.tensor.matmul(o, a, hid_hi[:, k, :], start=(k == 0), stop=False)
                            nc.tensor.matmul(o, a, hid_lo[:, k, :], start=False, stop=False)
                            last = nc.tensor.matmul(o, b, hid_hi[:, k, :], start=False, stop=(k == FT - 1))
                        if k == FT - 1:
                            last.then_inc(group_done, 1)
                for b in range(1, W2_BLOCKS):
                    split_ready(n0 + b, i * CHUNK_BLOCKS)
                    for d in range(2):
                        g = g0 + 2 * b + d
                        bank_free(g, i)
                        three_passes(g, (n0 + b) % SPLIT, lambda k: k * 2 * P + d * P, hid_hi, hid_lo, range(FT))

            def mlp(layer, half):
                first_of_all = (layer, half) == (0, 0)
                if not first_of_all:
                    pe.wait_ge(hn_ready, CHAIN["pool" if layer == 0 else "lstm", half] + 1)
                for a, b, what in segments(layer, half):
                    def chunk(i):
                        n0 = BLOCK["w1", layer, half, a, 0]
                        g0 = GROUPS["w1", layer, half, a, 0]
                        for f in range(W1_BLOCKS):
                            split_ready(n0 + f, i * CHUNK_BLOCKS)
                            bank_free(g0 + f, i)
                            follow = first_of_all and a == 0 and f == 0
                            three_passes(g0 + f, (n0 + f) % SPLIT, lambda k: k * P,
                                         hn_hi[half], hn_lo[half], range(KT),
                                         (lambda k: pe.wait_ge(hn0_tiles, k + 1)) if follow else None)
                        second_product(n0 + W1_BLOCKS, g0 + W1_BLOCKS, hid_tile(layer, half, a), i)

                    if b - a > 1:
                        with pe.Fori(0, b - a) as i:
                            chunk(i)
                    else:
                        chunk(0)
                    if what == "pool":
                        pool(1)

            def project(key, n, half):
                split_ready(n)
                bank_free(GROUPS[key])
                three_passes(GROUPS[key], n % SPLIT, lambda k: k * P, hn_hi[half], hn_lo[half], range(KT))

            def turn_gates(half):
                pe.wait_ge(gate_rows, half + 1)
                if half:
                    pe.wait_ge(hnorm_ready, HEADS * half)
                for c in range(CPH):
                    last = nc.tensor.transpose(core[3][:, c * P:(c + 1) * P], rows[:, c * LC:(c + 1) * LC], ident)
                last.then_inc(gate_cols, 1)

            def turn(j):
                pe.wait_ge(qk_ready, 2 * (j + 1))
                evacuated(pe, ("head", j, 2))
                if j:
                    pe.wait_ge(gated_ready, j)
                    pe.wait_ge(state_ready, j)
                    pe.wait_ge(hnorm_ready, j)
                for c in range(CPH):
                    s = slice(c * LC, (c + 1) * LC)
                    nc.tensor.transpose(core[0][:, s], kT[:, s], ident)
                for c in range(CPH):
                    s = slice(c * LC, (c + 1) * LC)
                    nc.tensor.transpose(core[1][:, s], vT[:, s], ident)
                for c in range(CPH):
                    s = slice(c * LC, (c + 1) * LC)
                    last = nc.tensor.matmul(core[2][:, s], kT[:, s], qT[:, j % 2, s], start=True, stop=True)
                last.then_inc(turned, 1)

            W = HEAD_DIM + 1

            def updates(j):
                pe.wait_ge(kw_ready, j + 1)
                pe.wait_ge(vtok_ready, j + 1)
                for c in range(CPH):
                    o = core[c // 2][:, (c % 2) * W:(c % 2 + 1) * W]
                    last = nc.tensor.matmul(o, kw[:, c * LC:(c + 1) * LC], v_tok[:, c, :], start=True, stop=True)
                last.then_inc(update_done, 1)

            def numerators(j):
                pe.wait_ge(prob_ready, j + 1)
                pe.wait_ge(qs_ready, j + 1)
                pe.wait_ge(gate_cols_ready, j // HEADS + 1)
                for c in range(CPH):
                    s = slice(c * LC, (c + 1) * LC)
                    o = core[2 + c // 2][:, (c % 2) * W:(c % 2 + 1) * W]
                    nc.tensor.matmul(o, prob[:, s], v_tok[:, c, :], start=True, stop=False)
                    if c:
                        pe.wait_ge(mid_ready, (CPH - 1) * j + c)
                    last = nc.tensor.matmul(o, qs[:, s], state[:, j % HEADS, :] if c == 0 else mid[:, c - 1, :],
                                            start=False, stop=True)
                last.then_inc(num_done, 1)

            def turn_back(j):
                pe.wait_ge(hnorm_ready, j + 1)
                pe.wait_ge(state_ready, j + 1)
                for c in range(CPH):
                    s = slice(c * LC, (c + 1) * LC)
                    last = nc.tensor.transpose(core[0][:, s], hnorm[:, s], ident)
                last.then_inc(hT_done, 1)

            def lstm():
                pe.wait_ge(vecs_in_s, 32)
                for j in range(STEPS + 1):
                    half = j // HEADS
                    g = heads_out(j)
                    if g is not None:
                        second_product(BLOCK["out", g, 0], GROUPS["out", g, 0], hid_tile("lstm", 0, g))
                    if j < STEPS and j % HEADS == 0:
                        pe.wait_ge(hn_ready, CHAIN["mlp0", half] + 1)
                        project(("gate", half), BLOCK["gate", half], half)
                    for t, work in enumerate((turn, updates, numerators, turn_back)):
                        if j < STEPS:
                            project(("head", j, t), BLOCK["head", j, t], half)
                        if t == 0 and j % HEADS == 1:
                            turn_gates(half)
                        if j:
                            work(j - 1)
                g = STEPS // FT - 1
                second_product(BLOCK["out", g, 0], GROUPS["out", g, 0], hid_tile("lstm", 0, g))

            pe.wait_ge(consts_set, 2)
            sum_squares(0)
            pool(0)
            sum_squares(1)
            sum_squares(2)
            mlp(0, 0)
            mlp(0, 1)
            lstm()
            mlp(1, 0)
            mlp(1, 1)
            sum_squares(15)

        def normed(eng, steps, outs, src, gain):
            g = vecs[:, gain:gain + 1]
            if eng is not nc.gpsimd:
                for o in outs:
                    ins = eng.scalar_tensor_tensor(out=o, in0=src, scalar=g, in1=rstd[:, :],
                                                   op0=ALU.mult, op1=ALU.mult)
                return ins
            steps.finish(eng.tensor_tensor(step_t[:, :], src, rstd[:, :], ALU.mult))
            for o in reversed(outs):
                ins = eng.tensor_scalar(o, step_t[:, :], g, 1.0, ALU.mult, ALU.mult)
            return ins

        def sum_of_squares(eng, steps, src, n):
            for k in range(KT):
                if k == 0:
                    steps.finish(eng.tensor_tensor(acc[:, :], src[:, k, :], src[:, k, :], ALU.mult))
                    continue
                steps.finish(eng.tensor_tensor(sq[:, :], src[:, k, :], src[:, k, :], ALU.mult))
                ins = eng.tensor_tensor(acc[:, :], acc[:, :], sq[:, :], ALU.add)
                if k < KT - 1:
                    steps.finish(ins)
            ins.then_inc(acc_ready, 1)

        def by(chain):
            if chain in (0, len(CHAINS) - 1):
                return "act", int(chain > 0)
            return "pool", chain - 1

        def xold_load(eng, chain, k):
            (_, half), _, _, source = CHAINS[chain]
            at = KT * chain + k
            if at >= 2:
                eng.wait_ge(xold_used, at - 1)
            src = x_in[half, k] if source == "input" else x_scratch[half, k]
            eng.dma_start(xold[:, at % 2, :], src).then_inc(xold_landed[by(chain)[0]][at % 2], 16)

        def xnew_store(eng, chain, k):
            (_, half), _, pre, _ = CHAINS[chain]
            eng.wait_ge(xnew_ready, KT * chain + k + 1)
            if pre is None:
                eng.dma_start(out[half, k], y[half][:, k, :]).then_inc(out_stored[by(chain)[0]], 16)
            else:
                eng.dma_start(x_scratch[half, k], y[half][:, k, :]).then_inc(stored[by(chain)[0]], 16)

        def add_residual(eng, steps, chain, dma):
            (_, half), post, _, _ = CHAINS[chain]
            eng.wait_ge(rstd_ready, NORM_POST[chain] + 1)
            if dma:
                xold_load(eng, chain, 0)
            for k in range(KT):
                if dma and k + 1 < KT:
                    xold_load(eng, chain, k + 1)
                at = KT * chain + k
                steps.finish(normed(eng, steps, [step_t[:, :]], y[half][:, k, :], post + k))
                who, before = by(chain)
                eng.wait_ge(xold_landed[who][at % 2], 16 * (before * KT // 2 + k // 2 + 1))
                eng.tensor_tensor(y[half][:, k, :], xold[:, at % 2, :], step_t[:, :], ALU.add).then_inc(xnew_ready, 1)
                eng.wait_ge(xnew_ready, at + 1)
                eng.sem_inc(xold_used, 1)
                if dma:
                    xnew_store(eng, chain, k)

        def norm_parts(eng, steps, half, gain, n):
            eng.wait_ge(rstd_ready, n + 1)
            for k in range(KT):
                steps.finish(normed(eng, steps, [step_t[:, :], hn_hi[half][:, k, :]], y[half][:, k, :], gain + k))
                steps.finish(eng.tensor_tensor(hn_lo[half][:, k, :], step_t[:, :],
                                               hn_hi[half][:, k, :].bitcast(F32), ALU.subtract))

        def chain_work(eng, steps, chain, dma):
            (_, half), _, pre, _ = CHAINS[chain]
            add_residual(eng, steps, chain, dma)
            if pre is not None:
                sum_of_squares(eng, steps, y[half], NORM_PRE[chain])

        def chain_end(eng, steps, chain):
            (_, half), _, pre, _ = CHAINS[chain]
            norm_parts(eng, steps, half, pre, NORM_PRE[chain])
            who, before = by(chain)
            eng.wait_ge(stored[who], 16 * KT * (before + 1))
            eng.sem_inc(hn_ready, 1)

        def first_norm_tile(eng, steps, half, k):
            at = KT * half + k
            if at >= 2:
                eng.wait_ge(xn_used, at - 1)
            if k:
                eng.wait_ge(xn_ready, at)
            normed(eng, steps, [craw[:, at % 2, HALO:]], y[half][:, k, :], V_MIX_PRE + k).then_inc(xn_ready, 1)

        @block.gpsimd
        def _(pool):
            steps = OwnSteps(pool, pool_own)

            def total(n):
                pool.wait_ge(acc_ready, n + 1 - 3)
                pool.wait_ge(rstd_ready, n)
                nc.gpsimd.partition_all_reduce(tot[:, :], acc[:, :], P, RADD).then_inc(tot_ready, 1)

            def background(chain):
                key, _, pre, _ = CHAINS[chain]
                half = key[1]
                evacuated(pool, LAST_GROUP[key])
                sum_of_squares(pool, steps, y[half], NORM_POST[chain])
                total(NORM_POST[chain])
                chain_work(pool, steps, chain, True)
                if pre is not None:
                    total(NORM_PRE[chain])
                    chain_end(pool, steps, chain)

            pool.memset(eps[:, :], EPS).then_inc(consts_set, 1)
            pool.memset(ones[:, :], 1.0).then_inc(consts_set, 1)
            pool.wait_ge(vecs_in_s, 32)
            pool.wait_ge(hn_ready, 1)
            pool.wait_ge(x_in_s[KT // 2], 16)
            sum_of_squares(pool, steps, y[1], NORM_FIRST[1])
            total(NORM_FIRST[1])
            pool.wait_ge(rstd_ready, NORM_FIRST[1] + 1)
            for k in range(KT):
                first_norm_tile(pool, steps, 1, k)
            for chain in range(1, len(CHAINS) - 1):
                background(chain)
            pool.wait_ge(out_stored["pool"], 16 * KT)

        @block.scalar
        def _(act):
            steps = OwnSteps(act, act_own)

            def split_hi(n, add=0, landed=0):
                if n >= NB:
                    return
                act.wait_ge(raw_landed[n % RAW], 16 * (n // RAW + 1) + landed)
                if n >= SPLIT:
                    act.wait_ge(group_done, BLOCK_END[n - SPLIT] + add)
                nc.scalar.copy(w_hi[:, n % SPLIT, :], raw[:, n % RAW, :]).then_inc(hi_ready, 1)

            def root(n):
                src = tot
                if n in FOREGROUND:
                    act.wait_ge(sq_summed, KT * (FOREGROUND.index(n) + 1))
                    src = core[3]
                    if n:
                        act.wait_ge(rstd_ready, n)
                else:
                    act.wait_ge(tot_ready, n + 1 - 3)
                nc.scalar.activation(tot[:, :], src[:, :], ACT.Sqrt, bias=eps[:, :], scale=1.0 / D).then_inc(std_ready, 1)

            def mlp(layer, half):
                for a, b, what in segments(layer, half):
                    n0 = BLOCK["w1", layer, half, a, 0]
                    g0 = GROUPS["w1", layer, half, a, 0]
                    t0 = hid_tile(layer, half, a)

                    def chunk(i):
                        for k in range(CHUNK_BLOCKS):
                            split_hi(n0 + k + 1, i * 12, i * (16 * CHUNK_BLOCKS // RAW))
                            if k >= W1_BLOCKS:
                                continue
                            act.wait_ge(group_done, g0 + k + 1 + i * 12)
                            if t0 + k >= 2:
                                act.wait_ge(hid_ready, t0 + k - 1 + i * FT)
                            r = relu[k % 2][:, :]
                            nc.scalar.activation(r, bank[(g0 + k) % BANKS][:, :], ACT.Relu).then_inc(evac_s["act"], 1)
                            act.wait_ge(evac_s["act"], EVAC[g0 + k][1] + i * EVACS["act"])
                            nc.scalar.activation(hid_hi[:, k, :], r, ACT.Square).then_inc(hidhi_ready, 1)

                    if b - a > 1:
                        with act.Fori(0, b - a) as i:
                            chunk(i)
                    else:
                        chunk(0)
                    if what == "pool":
                        for k in range(POOL_BLOCKS):
                            split_hi(BLOCK["pool", 1, k] + 1)
                    if what == "norm":
                        root(norms.pop(0))

            def gates(half):
                t = [y[half][0:HEADS, i, :] for i in range(8)]
                act.wait_ge(gate_z, half + 1)
                steps.finish(nc.scalar.activation(t[2], t[1], ACT.Abs))
                steps.finish(nc.scalar.activation(t[3], t[2], ACT.Exp, scale=-1.0))
                nc.scalar.activation(t[4], t[3], ACT.Ln, bias=1.0).then_inc(gate_l, 1)

            def gate_weights(half):
                t = [y[half][0:HEADS, i, :] for i in range(8)]
                act.wait_ge(gate_args, half + 1)
                if half:
                    act.wait_ge(gate_cols, half)
                nc.scalar.activation(rows[64:64 + HEADS, :], t[5], ACT.Exp)
                nc.scalar.activation(t[6], t[6], ACT.Exp)
                nc.scalar.activation(rows[96:96 + HEADS, :], t[7], ACT.Exp, scale=-1.0).then_inc(gate_exp, 1)
                act.wait_ge(gate_exp, half + 1)
                act.dma_start(row_scratch[half, 0], t[3]).then_inc(rows_stored, 16)
                act.dma_start(row_scratch[half, 1], rows[64:64 + HEADS, :]).then_inc(rows_stored, 16)

            def lstm():
                for j in range(STEPS + 1):
                    half = j // HEADS
                    g = heads_out(j)
                    if j in LSTM_NORM_STEPS:
                        root(norms.pop(0))
                    if g is not None:
                        for b in range(W2_BLOCKS):
                            split_hi(BLOCK["out", g, b] + 1)
                    if j % HEADS == 1:
                        act.wait_ge(rows_stored, 32 * (half + 1))
                        rows_to_all(j - 1)
                    if j == STEPS:
                        decay_matrix(j - 1)
                        by_tokens(j - 1)
                        head_norm(j - 1)
                        continue
                    if j % HEADS == 0:
                        split_hi(BLOCK["gate", half] + 1)
                    split_hi(BLOCK["head", j, 0] + 1)
                    conv_input(j, 0)
                    if j:
                        decay_matrix(j - 1)
                        by_tokens(j - 1)
                    split_hi(BLOCK["head", j, 1] + 1)
                    if j % HEADS == 0:
                        gates(half)
                    act.wait_ge(conv_ready, 2 * j + 1)
                    if j >= 2:
                        act.wait_ge(qs_ready, j - 1)
                        act.wait_ge(turned, j - 1)
                    nc.scalar.activation(qT[:, j % 2, :], win[:, 0, HALO:], ACT.Silu).then_inc(qk_ready, 1)
                    if j % HEADS:
                        rows_to_all(j)
                    conv_input(j, 1)
                    split_hi(BLOCK["head", j, 2] + 1)
                    act.wait_ge(conv_ready, 2 * j + 2)
                    nc.scalar.activation(kT[:, :], win[:, 1, HALO:], ACT.Silu).then_inc(qk_ready, 1)
                    act.wait_ge(group_done, GROUPS["head", j, 2] + 1)
                    nc.scalar.copy(vT[:, :], bank[GROUPS["head", j, 2] % BANKS][:, :]).then_inc(evac_s["act"], 1)
                    split_hi(BLOCK["head", j, 3] + 1)
                    if j:
                        head_squares(j - 1)
                        head_root(j - 1)
                    act.wait_ge(group_done, GROUPS["head", j, 3] + 1)
                    if j >= 2:
                        act.wait_ge(gated_ready, j - 1)
                    nc.scalar.activation(oT[:, j % 2, :], bank[GROUPS["head", j, 3] % BANKS][:, :],
                                         ACT.Sigmoid).then_inc(evac_s["act"], 1)
                    if j % HEADS == 0:
                        gate_weights(half)
                g = STEPS // FT - 1
                for b in range(W2_BLOCKS):
                    split_hi(BLOCK["out", g, b] + 1)

            def conv_input(j, t):
                act.wait_ge(group_done, GROUPS["head", j, t] + 1)
                if j:
                    act.wait_ge(conv_ready, 2 * j - 1 + t)
                nc.scalar.copy(craw[:, t, HALO:], bank[GROUPS["head", j, t] % BANKS][:, :]).then_inc(evac_s["act"], 1)

            def rows_to_all(j):
                if j >= 2:
                    act.wait_ge(prob_ready, j - 1)
                    act.wait_ge(state_ready, j - 1)
                    act.wait_ge(qs_ready, j - 1)
                for r, dst in enumerate((mx_b, inter_b)):
                    act.dma_start(dst[:, j % 2, :],
                                  row_scratch[j // HEADS, r, j % HEADS:j % HEADS + 1, :].to_broadcast([P, T])
                                  ).then_inc(bcast_landed[j % 2], 16)

            def decay_matrix(j):
                h, head = j // HEADS, j % HEADS
                act.wait_ge(mm_ready, j + 1)
                act.wait_ge(gate_cols_ready, h + 1)
                for c in range(CPH):
                    s = slice(c * LC, (c + 1) * LC)
                    last = nc.scalar.activation(mx_b[:, j % 2, s], mx_b[:, j % 2, s], ACT.Exp,
                                                bias=cols[:, h, c, head:head + 1])
                last.then_inc(decays, 1)

            def by_tokens(j):
                h, head = j // HEADS, j % HEADS
                act.wait_ge(turned, j + 1)
                if j:
                    act.wait_ge(num_done, j)
                for c in range(CPH):
                    s = slice(c * LC, (c + 1) * LC)
                    last = nc.scalar.activation(kw[:, s], core[0][:, s], ACT.Copy,
                                                scale=cols[:, h, c, 32 + head:33 + head])
                last.then_inc(kw_ready, 1)
                nc.scalar.copy(v_tok[:, :, 0:HEAD_DIM],
                               core[1][:, :].rearrange("p (c d) -> p c d", c=CPH)).then_inc(vtok_ready, 1)

            def head_squares(j):
                act.wait_ge(num_done, j + 1)
                if j:
                    act.wait_ge(hT_done, j)
                for c in range(CPH):
                    o = (c % 2) * (HEAD_DIM + 1)
                    last = nc.scalar.activation(hnorm[:, c * LC:(c + 1) * LC],
                                                core[2 + c // 2][:, o:o + HEAD_DIM], ACT.Square,
                                                accum_out=small[:, 0, c:c + 1])
                last.then_inc(ssq_ready, 1)

            def head_root(j):
                act.wait_ge(den_ready, j + 1)
                nc.scalar.activation(small[:, 6, :], small[:, 5, :], ACT.Sqrt, bias=eps[:, :],
                                     scale=1.0 / HEAD_DIM).then_inc(hstd_ready, 1)

            def head_norm(j):
                head_squares(j)
                head_root(j)

            def square(i, src):
                if i >= 4:
                    act.wait_ge(sq_summed, i - 3)
                nc.scalar.activation(squares[i % 4][:, :], src, ACT.Square).then_inc(sq_ready, 1)

            norms = list(range(16))
            act.dma_start(vecs[:, :], vecs_in).then_inc(vecs_in_s, 16)
            act.dma_start(consts[:, :], consts_in).then_inc(vecs_in_s, 16)
            for i in range(KT // 2):
                act.dma_start(y[0][:, 2 * i:2 * i + 2, :],
                              x_in[0, 2 * i:2 * i + 2].rearrange("k p t -> p k t")).then_inc(x_in_s[i], 16)
            act.dma_start(y[1][:, :, :], x_in[1].rearrange("k p t -> p k t")).then_inc(x_in_s[KT // 2], 16)
            for k in range(KT):
                if k % 2 == 0:
                    act.wait_ge(x_in_s[k // 2], 16)
                square(k, y[0][:, k, :])
            act.wait_ge(consts_set, 2)
            root(norms.pop(0))
            split_hi(0)
            act.wait_ge(bs_ready, 1)
            for b in range(POOL_BLOCKS):
                split_hi(b + 1)
                for d in range(4):
                    k = 4 * b + d
                    g = GROUPS["pool", 0, k]
                    act.wait_ge(group_done, g + 1)
                    nc.scalar.activation(y[0][:, k, :], bank[g % BANKS][:, :], ACT.Identity,
                                         bias=pool_bs[:, k:k + 1],
                                         scale=vecs[:, V_POOL_S + k:V_POOL_S + k + 1]).then_inc(evac_s["act"], 1)
                    act.wait_ge(evac_s["act"], EVAC[g][1])
                    square(KT + k, y[0][:, k, :])
            for k in range(2):
                xold_load(act, 0, k)
            root(norms.pop(0))
            for k in range(KT):
                xnew_store(act, 0, k)
                square(2 * KT + k, y[0][:, k, :])
                if k + 2 < KT:
                    xold_load(act, 0, k + 2)
            root(norms.pop(0))
            for k in range(KT):
                act.wait_ge(hn0_part, k + 1)
                nc.scalar.copy(hn_hi[0][:, k, :], parts[k % 2][:, :]).then_inc(hn0_hi, 1)
            mlp(0, 0)
            mlp(0, 1)
            lstm()
            mlp(1, 0)
            mlp(1, 1)
            last = len(CHAINS) - 1
            for k in range(KT):
                evacuated(act, ("w2", 1, 1, CHUNKS - 1, k))
                square(3 * KT + k, y[1][:, k, :])
            for k in range(2):
                xold_load(act, last, k)
            root(norms.pop(0))
            for k in range(KT):
                xnew_store(act, last, k)
                if k + 2 < KT:
                    xold_load(act, last, k + 2)
            act.wait_ge(out_stored["act"], 16 * KT)

        @block.vector
        def _(dve):
            steps = OwnSteps(dve, dve_own)
            norms = list(range(16))

            def split_lo(n, add_b=0, add_g=0):
                if n >= NB:
                    return
                dve.wait_ge(hi_ready, n + 1 + add_b)
                dve.tensor_tensor(w_lo[:, n % SPLIT, :], raw[:, n % RAW, :],
                                  w_hi[:, n % SPLIT, :].bitcast(F32), ALU.subtract).then_inc(lo_ready, 1)

            def reciprocal_root(n):
                dve.wait_ge(std_ready, n + 1)
                dve.reciprocal(rstd[:, :], tot[:, :]).then_inc(rstd_ready, 1)

            def windows(half, tiles):
                pooled = hnorm
                for k in tiles:
                    at = KT * half + k
                    src = craw[:, at % 2, :]
                    if half == 0:
                        first_norm_tile(dve, steps, 0, k)
                    dve.wait_ge(xn_ready, at + 1)
                    if half == 0:
                        steps.finish(dve.memset(src[:, 0:HALO], 0.0))
                    else:
                        steps.finish(dve.tensor_copy(src[:, 0:HALO], taps[:, k, :]))
                    if half == 0:
                        steps.finish(dve.tensor_copy(taps[:, k, :], src[:, T:T + HALO]))
                    g = k // 2
                    cur, w, lost = src, 1, 0
                    while w < WINDOWS[g]:
                        lost += w
                        nxt = win[:, (w.bit_length() + 1) % 2, :]
                        steps.finish(dve.tensor_tensor(nxt[:, lost:], cur[:, lost:], cur[:, lost - w:HALO + T - w],
                                                       ALU.add))
                        cur, w = nxt, 2 * w
                    steps.finish(dve.scalar_tensor_tensor(out=pooled[:, :], in0=cur[:, HALO:], scalar=1.0 / w,
                                                          in1=src[:, HALO:], op0=ALU.mult, op1=ALU.subtract))
                    if half == 0:
                        inv = consts[:, C_INV + g * HALO:C_INV + (g + 1) * HALO]
                        steps.finish(dve.tensor_tensor(cur[:, HALO:2 * HALO], cur[:, HALO:2 * HALO], inv, ALU.mult))
                        steps.finish(dve.tensor_tensor(pooled[:, 0:HALO], cur[:, HALO:2 * HALO],
                                                       src[:, HALO:2 * HALO], ALU.subtract))
                    steps.finish(dve.tensor_copy(hn_hi[half][:, k, :], pooled[:, :]))
                    steps.finish(dve.tensor_tensor(hn_lo[half][:, k, :], pooled[:, :],
                                                   hn_hi[half][:, k, :].bitcast(F32), ALU.subtract))
                    dve.sem_inc(xn_used, 1)
                    dve.sem_inc(pooled_ready, 1)

            def pool_out(half):
                for b in range(POOL_BLOCKS):
                    split_lo(BLOCK["pool", half, b] + 1)
                    for d in range(4):
                        k = 4 * b + d
                        g = GROUPS["pool", half, k]
                        dve.wait_ge(group_done, g + 1)
                        dve.tensor_scalar(y[half][:, k, :], bank[g % BANKS][:, :],
                                          vecs[:, V_POOL_B + k:V_POOL_B + k + 1],
                                          vecs[:, V_POOL_S + k:V_POOL_S + k + 1],
                                          ALU.add, ALU.mult).then_inc(evac_s["dve"], 1)

            def take_out(half, n0, g0, first, add_b=0, add_g=0, beside=None):
                for b in range(W2_BLOCKS):
                    split_lo(n0 + b + 1, add_b)
                    for d in range(2):
                        k = 2 * b + d
                        g = g0 + k
                        dve.wait_ge(group_done, g + 1 + add_g)
                        if first:
                            dve.tensor_copy(y[half][:, k, :], bank[g % BANKS][:, :]).then_inc(evac_s["dve"], 1)
                        else:
                            dve.tensor_tensor(y[half][:, k, :], bank[g % BANKS][:, :], y[half][:, k, :],
                                              ALU.add).then_inc(evac_s["dve"], 1)
                    if beside:
                        beside(W1_BLOCKS + b)

            def mlp(layer, half):
                for a, b, what in segments(layer, half):
                    n0 = BLOCK["w1", layer, half, a, 0]
                    g0 = GROUPS["w1", layer, half, a, 0]

                    t0 = hid_tile(layer, half, a)
                    m0 = (2 * layer + half) * CHUNKS * FT + a * FT

                    def beside(k):
                        if (layer, half) == (0, 0) and a in WINDOW_CHUNKS and k % 2:
                            tile = WINDOW_CHUNKS.index(a) * CHUNK_BLOCKS // 2 + k // 2
                            windows(1, [tile])

                    def chunk(i):
                        for f in range(W1_BLOCKS):
                            split_lo(n0 + f + 1, i * CHUNK_BLOCKS)
                            dve.wait_ge(evac_s["act"], EVAC[g0 + f][1] + i * EVACS["act"])
                            r = relu[f % 2][:, :]
                            if t0 + f:
                                dve.wait_ge(hid_ready, t0 + f + i * FT)
                            steps.finish(dve.tensor_tensor(relu_sq[:, :], r, r, ALU.mult))
                            dve.wait_ge(hidhi_ready, m0 + f + 1 + i * FT)
                            dve.tensor_tensor(hid_lo[:, f, :], relu_sq[:, :], hid_hi[:, f, :].bitcast(F32),
                                              ALU.subtract).then_inc(hid_ready, 1)
                            beside(f)
                        take_out(half, n0 + W1_BLOCKS, g0 + W1_BLOCKS, a == 0, i * CHUNK_BLOCKS, i * 12, beside)

                    if b - a > 1:
                        with dve.Fori(0, b - a) as i:
                            steps.repeat(i, W1_BLOCKS)
                            chunk(i)
                        steps.repeated(b - a)
                    else:
                        chunk(0)
                    if what == "pool":
                        pool_out(1)
                    if what == "norm":
                        reciprocal_root(norms.pop(0))

            def gates(half):
                t = [y[half][0:HEADS, i, :] for i in range(8)]
                g = GROUPS["gate", half]
                dve.wait_ge(group_done, g + 1)
                o = bank[g % BANKS]
                bi = V_GATE_B
                fr = GATE_ROW_F
                dve.tensor_scalar(t[1], o[fr:fr + HEADS, :], vecs[fr:fr + HEADS, bi:bi + 1], None,
                                  ALU.add).then_inc(gate_z, 1)
                steps.finish(dve.tensor_scalar(t[0], o[0:HEADS, :], vecs[0:HEADS, bi:bi + 1], None, ALU.add))
                dve.wait_ge(gate_z, half + 1)
                dve.sem_inc(evac_s["dve"], 1)

            def gate_chain(half):
                t = [y[half][0:HEADS, i, :] for i in range(8)]
                dve.wait_ge(gate_l, half + 1)
                steps.finish(dve.scalar_tensor_tensor(out=t[4], in0=t[1], scalar=0.0, in1=t[4],
                                                      op0=ALU.min, op1=ALU.subtract))
                for c in range(CPH):
                    s = slice(c * LC, (c + 1) * LC)
                    ins = dve.tensor_tensor_scan(t[2][:, s], zrow[:, :], t[4][:, s], 0.0, ALU.add, ALU.add)
                steps.finish(ins)
                steps.finish(dve.tensor_tensor(t[0], t[0], t[2], ALU.subtract))
                for c in range(CPH):
                    s = slice(c * LC, (c + 1) * LC)
                    e = (c + 1) * LC
                    i = half * CPH + c
                    steps.finish(dve.tensor_tensor_scan(t[3][:, s], zrow[:, :], t[0][:, s], m_run[:, i:i + 1],
                                                        ALU.add, ALU.max))
                    steps.finish(dve.tensor_tensor(m_run[:, i + 1:i + 2], t[3][:, e - 1:e], t[2][:, e - 1:e], ALU.add))
                    dve.tensor_scalar(t[5][:, s], t[3][:, s], -1.0, m_run[:, i:i + 1], ALU.mult, ALU.add)
                    ins = dve.tensor_scalar(t[6][:, s], t[0][:, s], t[3][:, e - 1:e], None, ALU.subtract)
                steps.finish(ins)
                dve.tensor_tensor(t[7], t[2], t[3], ALU.add).then_inc(gate_args, 1)

            def gate_tail(half):
                t = [y[half][0:HEADS, i, :] for i in range(8)]
                dve.wait_ge(gate_exp, half + 1)
                dve.tensor_copy(rows[0:HEADS, :], t[0])
                steps.finish(dve.tensor_scalar(rows[32:32 + HEADS, :], t[6], KSCALE, None, ALU.mult))
                dve.sem_inc(gate_rows, 1)

            def gate_columns(half):
                dve.wait_ge(gate_cols, half + 1)
                dve.tensor_copy(cols[:, half, :, :].rearrange("p c r -> p (c r)"), core[3][:, :]).then_inc(gate_cols_ready, 1)

            def conv(j, t):
                tile = t * HEADS + j % HEADS
                src = craw[:, t, :]
                dve.wait_ge(evac_s["act"], EVAC[GROUPS["head", j, t]][1])
                steps.finish(dve.tensor_copy(src[:, 0:HALO], taps[:, tile, :]))
                dve.tensor_copy(taps[:, tile, :], src[:, T:T + HALO])
                if j:
                    dve.wait_ge(qk_ready, 2 * j - 1 + t)
                dst = win[:, t, HALO:]
                for i in range(TAPS):
                    lag = TAPS - 1 - i
                    w = vecs[:, V_CONV_W + i * 2 * HEADS + tile:V_CONV_W + i * 2 * HEADS + tile + 1]
                    view = src[:, HALO - lag:HALO + T - lag]
                    if i == 0:
                        steps.finish(dve.tensor_scalar(dst, view, w, vecs[:, V_CONV_B + tile:V_CONV_B + tile + 1],
                                                       ALU.mult, ALU.add))
                    elif i < TAPS - 1:
                        steps.finish(dve.scalar_tensor_tensor(out=dst, in0=view, scalar=w, in1=dst,
                                                              op0=ALU.mult, op1=ALU.add))
                    else:
                        dve.scalar_tensor_tensor(out=dst, in0=view, scalar=w, in1=dst,
                                                 op0=ALU.mult, op1=ALU.add).then_inc(conv_ready, 1)

            def probabilities(j):
                dve.wait_ge(turned, j + 1)
                dve.wait_ge(decays, j + 1)
                if j:
                    dve.wait_ge(num_done, j)
                dve.scalar_tensor_tensor(out=prob[:, :], in0=core[2][:, :], scalar=KSCALE, in1=mx_b[:, j % 2, :],
                                         op0=ALU.mult, op1=ALU.mult).then_inc(prob_ready, 1)

            def states(j):
                dve.wait_ge(update_done, j + 1)
                if j:
                    dve.wait_ge(num_done, j)
                for c in range(CPH - 1):
                    state_after(j, c).then_inc(mid_ready, 1)
                    dve.wait_ge(mid_ready, (CPH - 1) * j + c + 1)

            def state_after(j, c):
                o = core[c // 2][:, (c % 2) * (HEAD_DIM + 1):(c % 2 + 1) * (HEAD_DIM + 1)]
                e = (c + 1) * LC
                before = state[:, j % HEADS, :] if c == 0 else mid[:, c - 1, :]
                after = mid[:, c, :] if c < CPH - 1 else state[:, j % HEADS, :]
                return dve.scalar_tensor_tensor(out=after, in0=before, scalar=inter_b[:, j % 2, e - 1:e], in1=o,
                                                op0=ALU.mult, op1=ALU.add)

            def normalize(j, between):
                h, head = j // HEADS, j % HEADS
                dve.wait_ge(num_done, j + 1)
                state_after(j, CPH - 1).then_inc(state_ready, 1)
                dve.wait_ge(ssq_ready, j + 1)
                for b in range(2):
                    den = core[2 + b][:, 0:2 * (HEAD_DIM + 1)].rearrange("p (c w) -> p c w", c=2)[:, :, HEAD_DIM:HEAD_DIM + 1]
                    ins = dve.tensor_copy(small[:, 1, 2 * b:2 * b + 2].rearrange("p (c o) -> p c o", o=1), den)
                steps.finish(ins)
                steps.finish(dve.scalar_tensor_tensor(out=small[:, 2, :], in0=small[:, 1, :], scalar=-1.0,
                                                      in1=small[:, 1, :], op0=ALU.mult, op1=ALU.max))
                steps.finish(dve.tensor_tensor(small[:, 3, :], small[:, 2, :], cols[:, h, :, 96 + head], ALU.max))
                steps.finish(dve.reciprocal(small[:, 4, :], small[:, 3, :]))
                steps.finish(dve.tensor_tensor(small[:, 1, :], small[:, 0, :], small[:, 4, :], ALU.mult))
                dve.tensor_tensor(small[:, 5, :], small[:, 1, :], small[:, 4, :], ALU.mult).then_inc(den_ready, 1)
                between()
                dve.wait_ge(hstd_ready, j + 1)
                steps.finish(dve.reciprocal(small[:, 7, :], small[:, 6, :]))
                steps.finish(dve.tensor_tensor(small[:, 7, :], small[:, 7, :], small[:, 4, :], ALU.mult))
                for c in range(CPH):
                    o = (c % 2) * (HEAD_DIM + 1)
                    ins = dve.tensor_scalar(hnorm[:, c * LC:(c + 1) * LC], core[2 + c // 2][:, o:o + HEAD_DIM],
                                            small[:, 7, c:c + 1], None, ALU.mult)
                ins.then_inc(hnorm_ready, 1)

            def gate_head(j):
                k = j % HEADS
                dve.wait_ge(hT_done, j + 1)
                dve.wait_ge(evac_s["act"], EVAC[GROUPS["head", j, 3]][1])
                steps.finish(dve.scalar_tensor_tensor(out=relu_sq[:, :], in0=core[0][:, :],
                                                      scalar=vecs[:, V_HEAD_NORM + k:V_HEAD_NORM + k + 1],
                                                      in1=oT[:, j % 2, :], op0=ALU.mult, op1=ALU.mult))
                dve.sem_inc(gated_ready, 1)
                steps.finish(dve.tensor_copy(hid_hi[:, j % FT, :], relu_sq[:, :]))
                dve.tensor_tensor(hid_lo[:, j % FT, :], relu_sq[:, :], hid_hi[:, j % FT, :].bitcast(F32),
                                  ALU.subtract).then_inc(hid_ready, 1)

            def rows_for(j):
                dve.wait_ge(bcast_landed[j % 2], 32 * (j // 2 + 1))
                dve.tensor_tensor(mx_b[:, j % 2, :], mask, mx_b[:, j % 2, :], ALU.subtract).then_inc(mm_ready, 1)
                dve.wait_ge(qk_ready, 2 * j + 1)
                if j:
                    dve.wait_ge(num_done, j)
                dve.tensor_tensor(qs[:, :], qT[:, j % 2, :], inter_b[:, j % 2, :], ALU.mult).then_inc(qs_ready, 1)

            def lstm():
                steps.finish(dve.memset(taps[:, :, :], 0.0))
                for j in range(STEPS + 1):
                    half = j // HEADS
                    g = heads_out(j)
                    if j in LSTM_NORM_STEPS:
                        reciprocal_root(norms.pop(0))
                    if g is not None:
                        take_out(g // 2, BLOCK["out", g, 0], GROUPS["out", g, 0], g % 2 == 0)
                    if j == STEPS:
                        probabilities(j - 1)
                        states(j - 1)
                        normalize(j - 1, lambda: None)
                        gate_head(j - 1)
                        continue
                    if j % HEADS == 0:
                        split_lo(BLOCK["gate", half] + 1)
                        gates(half)
                    split_lo(BLOCK["head", j, 0] + 1)
                    if j % HEADS == 1:
                        rows_for(j - 1)
                    conv(j, 0)
                    if j % HEADS == 1:
                        gate_columns(half)
                    if j:
                        probabilities(j - 1)
                    split_lo(BLOCK["head", j, 1] + 1)
                    if j % HEADS == 0:
                        gate_chain(half)
                    if j:
                        states(j - 1)
                    conv(j, 1)
                    split_lo(BLOCK["head", j, 2] + 1)
                    if j % HEADS:
                        rows_for(j)
                    if j:
                        normalize(j - 1, lambda: split_lo(BLOCK["head", j, 3] + 1))
                        gate_head(j - 1)
                    else:
                        split_lo(BLOCK["head", j, 3] + 1)
                    if j % HEADS == 0:
                        gate_tail(half)
                g = STEPS // FT - 1
                take_out(g // 2, BLOCK["out", g, 0], GROUPS["out", g, 0], g % 2 == 0)

            dve.memset(state[:, :, :], 0.0)
            dve.memset(rows[:, :], 0.0)
            dve.memset(zrow[:, :], 0.0)
            dve.memset(m_run[:, 0:1], 0.0)
            steps.finish(dve.memset(v_tok[:, :, HEAD_DIM:], 1.0))
            dve.wait_ge(vecs_in_s, 32)
            dve.tensor_tensor(pool_bs[:, :], vecs[:, V_POOL_B:V_POOL_B + KT], vecs[:, V_POOL_S:V_POOL_S + KT],
                              ALU.mult).then_inc(bs_ready, 1)
            reciprocal_root(norms.pop(0))
            dve.wait_ge(rstd_ready, 1)
            split_lo(0)
            windows(0, range(KT))
            for b in range(POOL_BLOCKS):
                split_lo(b + 1)
            reciprocal_root(norms.pop(0))
            add_residual(dve, steps, 0, False)
            reciprocal_root(norms.pop(0))
            dve.wait_ge(rstd_ready, 3)
            for k in range(KT + 1):
                if k < KT:
                    normed(dve, steps, [parts[k % 2][:, :]], y[0][:, k, :], V_FFN_PRE + k).then_inc(hn0_part, 1)
                if k:
                    dve.wait_ge(hn0_hi, k)
                    dve.wait_ge(hn0_part, k)
                    dve.tensor_tensor(hn_lo[0][:, k - 1, :], parts[(k - 1) % 2][:, :],
                                      hn_hi[0][:, k - 1, :].bitcast(F32), ALU.subtract).then_inc(hn0_tiles, 1)
                    dve.wait_ge(hn0_tiles, k)
            who, before = by(0)
            dve.wait_ge(stored[who], 16 * KT)
            dve.sem_inc(hn_ready, 1)
            mlp(0, 0)
            mlp(0, 1)
            lstm()
            mlp(1, 0)
            mlp(1, 1)
            last = len(CHAINS) - 1
            reciprocal_root(norms.pop(0))
            add_residual(dve, steps, last, False)


def kernel(x, mix_pre_g, mix_post_g, ffn_pre_g, ffn_post_g, pool_w, pool_b, pool_scale,
           mlstm_w_in, mlstm_conv_w, mlstm_conv_b, mlstm_i_bias, mlstm_f_bias,
           mlstm_head_norm_w, mlstm_w_out, mlp_w1, mlp_w2):
    import concourse.bacc as bacc
    from concourse.bass_utils import run_bass_kernel_spmd

    def tiles_of(w, rows, columns):
        n = w.shape[1] // columns
        return w.reshape(rows, P, n, columns).transpose(2, 1, 0, 3).reshape(n, P, rows * columns)

    def mlp_blocks(w1, w2):
        first = tiles_of(w1, KT, P)
        out = []
        for c in range(CHUNKS):
            out.append(first[c * FT:(c + 1) * FT])
            out.append(tiles_of(w2[c * FT * P:(c + 1) * FT * P], FT, 2 * P))
        return out

    x, pool_w, w_in, w_out = (np.asarray(a) for a in (x, pool_w, mlstm_w_in, mlstm_w_out))
    w1, w2 = np.asarray(mlp_w1), np.asarray(mlp_w2)
    pool_blocks = pool_w[0].reshape(2, 2, 2, P, GROUP).transpose(0, 3, 1, 2, 4).reshape(2, P, BLK)
    gate_block = np.zeros((P, KT, P), np.float32)
    gates = w_in[0][:, 4 * D:].reshape(KT, P, 2 * HEADS).transpose(1, 0, 2)
    gate_block[:, :, 0:HEADS] = gates[:, :, 0:HEADS]
    gate_block[:, :, GATE_ROW_F:GATE_ROW_F + HEADS] = gates[:, :, HEADS:]
    heads = tiles_of(w_in[0][:, :4 * D], KT, P).reshape(HEAD_BLOCKS, HEADS, P, BLK).transpose(1, 0, 2, 3)
    outs = [tiles_of(w_out[0][g * FT * P:(g + 1) * FT * P], FT, 2 * P) for g in range(2)]
    stream = np.concatenate([pool_blocks, *mlp_blocks(w1[0], w2[0]), gate_block.reshape(1, P, BLK),
                             heads.reshape(-1, P, BLK), *outs, *mlp_blocks(w1[1], w2[1])])
    assert stream.shape == (DRAM_BLOCKS, P, BLK)

    columns = [np.asarray(a).reshape(-1, P).T for a in (
        mix_pre_g, mix_post_g, ffn_pre_g, ffn_post_g, pool_b, pool_scale, mlstm_conv_w, mlstm_conv_b,
        mlstm_head_norm_w)]
    biases = np.zeros((P, 1), np.float32)
    biases[0:HEADS, 0] = np.asarray(mlstm_i_bias)[0]
    biases[GATE_ROW_F:GATE_ROW_F + HEADS, 0] = np.asarray(mlstm_f_bias)[0]
    vectors = np.ascontiguousarray(np.concatenate([*columns, biases], axis=1))
    assert vectors.shape == (P, VECS)

    at = np.arange(P)
    causal = np.where(at[:, None] <= at[None, :], 0.0, NEG).astype(np.float32)
    first = np.concatenate([1.0 / np.minimum(np.arange(HALO) + 1, w) for w in WINDOWS]).astype(np.float32)
    constants = np.concatenate([np.eye(P, dtype=np.float32), *[causal] * CPH,
                                np.broadcast_to(first, (P, first.size))], axis=1)

    x_tiles = np.ascontiguousarray(x[0].T.reshape(KT, P, HALVES, T).transpose(2, 0, 1, 3))
    arrays = {"x_tiles": x_tiles, "weights": np.ascontiguousarray(stream), "vectors": vectors,
              "constants": np.ascontiguousarray(constants)}

    nc = bacc.Bacc("TRN2", target_bir_lowering=False, num_devices=1)
    args = [nc.dram_tensor(name, a.shape, F32, kind="ExternalInput").ap() for name, a in arrays.items()]
    out = nc.dram_tensor("out_tiles", x_tiles.shape, F32, kind="ExternalOutput").ap()
    build(nc, *args, out)
    result = run_bass_kernel_spmd(nc, [arrays], core_ids=[0]).results[0]["out_tiles"]
    return result.transpose(1, 2, 0, 3).reshape(1, D, SEQ).transpose(0, 2, 1)
```

```python
from contextlib import ExitStack

import numpy as np

import concourse.bass as bass
from concourse import mybir

ALU = mybir.AluOpType
ACT = mybir.ActivationFunctionType
F32 = mybir.dt.float32
F32R = mybir.dt.float32r
RADD = bass.bass_isa.ReduceOp.add

P = 128
D = 1024
SEQ = 1024
HALVES = 2
T = SEQ // HALVES
KT = D // P
D_FF = 4 * D
HEADS = 8
HEAD_DIM = D // HEADS
TAPS = 4
LC = 128
CPH = T // LC
WINDOWS = (2, 4, 8, 16)
GROUP = D // len(WINDOWS)
HALO = 16
EPS = 1e-6
KSCALE = HEAD_DIM ** -0.5
NEG = -1e30

BLK = 8 * P
FT = 4
W1_BLOCKS = FT
W2_BLOCKS = KT // 2
CHUNK_BLOCKS = W1_BLOCKS + W2_BLOCKS
CHUNKS = D_FF // (FT * P)
POOL_BLOCKS = 2
HEAD_BLOCKS = 4
GATE_ROW_F = 32
D_POOL = 0
D_MLP = (POOL_BLOCKS, POOL_BLOCKS + CHUNKS * CHUNK_BLOCKS + 1 + HEADS * HEAD_BLOCKS + 2 * W2_BLOCKS)
D_GATE = D_MLP[0] + CHUNKS * CHUNK_BLOCKS
D_HEAD = D_GATE + 1
D_OUT = D_HEAD + HEADS * HEAD_BLOCKS
DRAM_BLOCKS = D_MLP[1] + CHUNKS * CHUNK_BLOCKS

RAW = 2
SPLIT = 2
BANKS = 4
STEPS = HALVES * HEADS

V_MIX_PRE, V_MIX_POST, V_FFN_PRE, V_FFN_POST = 0, 16, 32, 48
V_POOL_B, V_POOL_S = 64, 72
V_CONV_W, V_CONV_B = 80, 144
V_HEAD_NORM, V_GATE_B = 160, 168
VECS = 169
C_IDENT, C_MASK = 0, P
CONSTS = P + T
NW = len(WINDOWS)
B_SELF, B_NEXT, B_FIRST = 0, NW * P, NW * (P + HALO)
BANDS = NW * (P + 2 * HALO)

MLP_INTERLUDES = {
    (0, 0): {0: "norm", 2: "norm"},
    (0, 1): {0: "norm", 2: "norm"},
    (1, 0): {0: "norm", 2: "norm"},
    (1, 1): {0: "norm"},
}
LSTM_NORM_STEPS = (2, 5, 11, 14)
SECOND_POOL = ("W3 W4 W5 W6 W7 G0 G1 G2 G3 S0 S1 S2 S3 S4 S5 G4 G5 S6 S7 G6 G7").split()


def segments(layer, half):
    marks = MLP_INTERLUDES[layer, half]
    last = {CHUNKS - 2} if (layer, half) == (1, 1) else set()
    cuts = sorted({0, CHUNKS - 1, *marks, *last})
    out, at = [], 0
    for c in cuts:
        out.append((at, c + 1, marks.get(c)))
        at = c + 1
    return out


def heads_out(j):
    return j // FT - 1 if j > FT and j % FT == 1 else None


def plan():
    p = {"block": {}, "dram": [], "group": {}, "evac": [], "block_end": []}
    evacs = {"dve": 0, "act": 0}

    def block(key, dram):
        p["block"][key] = len(p["dram"])
        p["dram"].append(dram)

    def group(key, engine):
        p["group"][key] = len(p["evac"])
        evacs[engine] += 1
        p["evac"].append((engine, evacs[engine]))

    def block_ends():
        p["block_end"].append(len(p["evac"]))

    def pool():
        for b in range(POOL_BLOCKS):
            block(("pool", b), D_POOL + b)
        for half in range(HALVES):
            for d in range(KT):
                group(("pool", half, d), "act")
        for b in range(POOL_BLOCKS):
            p["block_end"].append(KT + 4 * (b + 1))

    def mlp(layer, half):
        for c in range(CHUNKS):
            for f in range(W1_BLOCKS):
                block(("w1", layer, half, c, f), D_MLP[layer] + c * CHUNK_BLOCKS + f)
                group(("w1", layer, half, c, f), "act")
                block_ends()
            for b in range(W2_BLOCKS):
                block(("w2", layer, half, c, b), D_MLP[layer] + c * CHUNK_BLOCKS + W1_BLOCKS + b)
                for d in range(2):
                    group(("w2", layer, half, c, 2 * b + d), "dve")
                block_ends()

    def project_out(g):
        for b in range(W2_BLOCKS):
            block(("out", g, b), D_OUT + (g % 2) * W2_BLOCKS + b)
            for d in range(2):
                group(("out", g, 2 * b + d), "dve")
            block_ends()

    pool()
    mlp(0, 0)
    mlp(0, 1)
    for j in range(STEPS):
        if heads_out(j) is not None:
            project_out(heads_out(j))
        if j % HEADS == 0:
            block(("gate", j // HEADS), D_GATE)
            group(("gate", j // HEADS), "dve")
            block_ends()
        for t in range(HEAD_BLOCKS):
            block(("head", j, t), D_HEAD + (j % HEADS) * HEAD_BLOCKS + t)
            group(("head", j, t), "act")
            block_ends()
    project_out(STEPS // FT - 1)
    mlp(1, 0)
    mlp(1, 1)
    return p


class OwnSteps:

    def __init__(self, engine, sem):
        self.engine, self.sem, self.n, self.loop = engine, sem, 0, 0

    def begin(self, ins):
        self.n += 1
        ins.then_inc(self.sem, 1)
        return self.n

    def end(self, n):
        self.engine.wait_ge(self.sem, n + self.loop)

    def finish(self, ins):
        self.end(self.begin(ins))

    def repeat(self, i, per):
        self.loop = i * per
        self.start, self.per = self.n, per

    def repeated(self, times):
        assert self.n - self.start == self.per, (self.n - self.start, self.per)
        self.n, self.loop = self.start + self.per * times, 0


def build(nc, x_in, x_tokens, weights, vecs_in, consts_in, bands_in, out):
    plan_ = plan()
    BLOCK, DRAM, GROUPS, EVAC, BLOCK_END = (
        plan_["block"], plan_["dram"], plan_["group"], plan_["evac"], plan_["block_end"])
    NB = len(DRAM)

    with ExitStack() as ctx:
        def sb(name, shape, dt=F32):
            return ctx.enter_context(nc.sbuf_tensor(name, shape, dt))

        def psum(name, shape):
            return ctx.enter_context(nc.psum_tensor(name, shape, F32))

        def sem(name):
            return ctx.enter_context(nc.semaphore(name))

        hn_hi = [sb(f"hn_hi{h}", [P, KT, T], F32R) for h in range(HALVES)]
        hn_lo = [sb(f"hn_lo{h}", [P, KT, T], F32R) for h in range(HALVES)]
        y = [sb(f"y{h}", [P, KT, T]) for h in range(HALVES)]
        hid_hi = sb("hid_hi", [P, FT, T], F32R)
        hid_lo = sb("hid_lo", [P, FT, T], F32R)
        raw = sb("raw", [P, RAW, BLK])
        w_hi = sb("w_hi", [P, SPLIT, BLK], F32R)
        w_lo = sb("w_lo", [P, SPLIT, BLK], F32R)
        vecs = sb("vecs", [P, VECS])
        consts = sb("consts", [P, CONSTS])
        ident = consts[:, C_IDENT:C_IDENT + P]
        mask = consts[:, C_MASK:C_MASK + T]
        eps = sb("eps", [P, 1])
        sq = sb("sq", [P, T])
        acc = sb("acc", [P, T])
        tot = sb("tot", [P, T])
        rstd = sb("rstd", [P, T])
        xold = sb("xold", [P, 2, T])
        step_t = sb("step_t", [P, T])
        relu_sq = sb("relu_sq", [P, T])
        ones = sb("ones", [P, P])
        pool_bs = sb("pool_bs", [P, KT])
        craw = sb("craw", [P, 2, HALO + T])
        taps = sb("taps", [P, 2 * HEADS, HALO])
        win = sb("win", [P, 2, HALO + T])
        qT = sb("qT", [P, 2, T])
        kT = sb("kT", [P, T])
        vT = sb("vT", [P, T])
        oT = sb("oT", [P, 2, T])
        mx_b = sb("mx_b", [P, 2, T])
        inter_b = sb("inter_b", [P, 2, T])
        qs = sb("qs", [P, T])
        kw = sb("kw", [P, T])
        v_tok = sb("v_tok", [P, CPH, HEAD_DIM + 1])
        prob = sb("prob", [P, T])
        hnorm = sb("hnorm", [P, T])
        state = sb("state", [P, HEADS, HEAD_DIM + 1])
        mid = sb("mid", [P, CPH - 1, HEAD_DIM + 1])
        rows = sb("rows", [P, T])
        cols = sb("cols", [P, 2, CPH, P])
        small = sb("small", [P, 8, CPH])
        zrow = sb("zrow", [HEADS, LC])
        m_run = sb("m_run", [HEADS, STEPS])

        relu = [kw, prob]

        parts = [inter_b[:, 0, :], inter_b[:, 1, :]]
        ones_row = relu_sq
        squares = [qs[:, :], vT[:, :], kT[:, :], oT[:, 0, :], oT[:, 1, :], hnorm[:, :],
                   craw[:, 0, 0:T], craw[:, 1, 0:T]]
        token_sq = mx_b[:, :, :].rearrange("p a t -> p (a t)")
        x_halo = qT[:, :, :].rearrange("p a t -> p (a t)")
        ssq = sb("ssq", [P, 2, HALVES * CPH])
        rs = sb("rs", [P, HALVES * CPH])
        band_consts = cols[:, :, :, :].rearrange("p h c r -> p (h c r)")[:, 0:BANDS]
        self_band = [kw[:, :], prob[:, :], sq[:, :], acc[:, :]]
        next_band = [win[:, i // CPH, (i % CPH) * NW * HALO:(i % CPH + 1) * NW * HALO] for i in range(HALVES * CPH)]

        def x_tok(half, c):
            if half == 1 and c < 0:
                return x_halo
            return y[half][:, 2 * c:2 * c + 2, :].rearrange("p a t -> p (a t)")

        bank = [psum(f"bank{i}", [P, T]) for i in range(BANKS)]
        core = [psum(f"core{i}", [P, T]) for i in range(4)]

        x_scratch = nc.dram_tensor("x_scratch", [HALVES, KT, P, T], F32).ap()
        row_scratch = nc.dram_tensor("row_scratch", [HALVES, 2, HEADS, T], F32).ap()

        vecs_in_s = sem("vectors_landed")
        x_tok_s = [sem(f"x_tokens_landed{i}") for i in range(HALVES * CPH)]
        bands_in_s = sem("band_constants_landed")
        x_halo_s = sem("x_halo_landed")
        tok_std = sem("token_roots_ready")
        bands_ready = sem("bands_ready")
        windows_done = sem("windows_done")
        pooled_hi = sem("pooled_high_ready")
        bs_ready = sem("pool_bias_ready")
        sq_ready = sem("square_ready")
        sq_summed = sem("square_summed")
        hn0_part = sem("hn0_part_ready")
        hn0_hi = sem("hn0_high_ready")
        hn0_tiles = sem("hn0_tiles_ready")
        hidhi_ready = sem("hidden_high_ready")
        consts_set = sem("consts_set")
        raw_landed = [sem(f"raw_landed{i}") for i in range(RAW)]
        hi_ready = sem("w_hi_ready")
        lo_ready = sem("w_lo_ready")
        group_done = sem("group_done")
        evac_s = {"dve": sem("evac_dve"), "act": sem("evac_act")}
        hid_ready = sem("hidden_ready")
        hn_ready = sem("hn_ready")
        pooled_ready = sem("pooled_ready")
        acc_ready = sem("acc_ready")
        tot_ready = sem("total_ready")
        std_ready = sem("std_ready")
        rstd_ready = sem("rstd_ready")
        xold_landed = {w: [sem(f"xold_landed_{w}{i}") for i in range(2)] for w in ("act", "pool")}
        x_last_landed = sem("last_old_x_landed")
        xold_used = sem("xold_used")
        xnew_ready = sem("xnew_ready")
        stored = {w: sem(f"x_stored_{w}") for w in ("act", "pool")}
        out_stored = {w: sem(f"out_stored_{w}") for w in ("act", "pool")}
        dve_own = sem("dve_own")
        act_own = sem("act_own")
        pool_own = sem("pool_own")
        conv_ready = sem("conv_ready")
        qk_ready = sem("qk_ready")
        gate_z = sem("gate_z")
        gate_l = sem("gate_l")
        gate_args = sem("gate_args")
        gate_exp = sem("gate_exp")
        gate_rows = sem("gate_rows")
        gate_cols = sem("gate_cols")
        gate_cols_ready = sem("gate_cols_ready")
        rows_stored = sem("rows_stored")
        bcast_landed = [sem(f"bcast_landed{i}") for i in range(2)]
        mm_ready = sem("masked_max_ready")
        qs_ready = sem("qs_ready")
        turned = sem("core_turned")
        decays = sem("decay_matrix_ready")
        kw_ready = sem("kw_ready")
        vtok_ready = sem("v_tok_ready")
        prob_ready = sem("prob_ready")
        update_done = sem("state_updates_done")
        mid_ready = sem("mid_state_ready")
        state_ready = sem("state_ready")
        num_done = sem("numerators_done")
        ssq_ready = sem("head_ssq_ready")
        den_ready = sem("den_ready")
        hstd_ready = sem("head_std_ready")
        hnorm_ready = sem("hnorm_ready")
        hT_done = sem("head_turned_back")
        gated_ready = sem("gated_used")

        block = ctx.enter_context(nc.Block())

        CHAINS = [
            (("pool", 0), V_MIX_POST, V_FFN_PRE, "input"),
            (("pool", 1), V_MIX_POST, V_FFN_PRE, "input"),
            (("mlp0", 0), V_FFN_POST, V_MIX_PRE + 8, "scratch"),
            (("mlp0", 1), V_FFN_POST, V_MIX_PRE + 8, "scratch"),
            (("lstm", 0), V_MIX_POST + 8, V_FFN_PRE + 8, "scratch"),
            (("lstm", 1), V_MIX_POST + 8, V_FFN_PRE + 8, "scratch"),
            (("mlp1", 0), V_FFN_POST + 8, None, "scratch"),
            (("mlp1", 1), V_FFN_POST + 8, None, "scratch"),
        ]
        CHAIN = {key: n for n, (key, *_) in enumerate(CHAINS)}
        LAST_GROUP = {
            ("pool", 0): ("pool", 0, 7), ("pool", 1): ("pool", 1, 7),
            ("mlp0", 0): ("w2", 0, 0, CHUNKS - 1, 7), ("mlp0", 1): ("w2", 0, 1, CHUNKS - 1, 7),
            ("lstm", 0): ("out", 1, 7), ("lstm", 1): ("out", 3, 7),
            ("mlp1", 0): ("w2", 1, 0, CHUNKS - 1, 7), ("mlp1", 1): ("w2", 1, 1, CHUNKS - 1, 7),
        }
        NORM_POST = (0, 2, 4, 6, 8, 10, 12, 13)
        NORM_PRE = (1, 3, 5, 7, 9, 11)
        NORMS = 14
        FOREGROUND = (0, 1, 13)
        BACKGROUND = 2
        EVACS = {"act": W1_BLOCKS, "dve": KT}

        def evacuated(eng, key, add=0):
            who, count = EVAC[GROUPS[key]]
            eng.wait_ge(evac_s[who], count + add)

        def hid_tile(layer, half, c):
            per = CHUNKS * FT
            if layer == "lstm":
                return 2 * per + FT * c
            return (2 * per + STEPS if layer else 0) + half * per + FT * c

        @block.sync
        def _(sp):
            def load(n, dram, loop_blocks=0):
                if n >= RAW:
                    sp.wait_ge(hi_ready, n - RAW + 1 + loop_blocks)
                    sp.wait_ge(lo_ready, n - RAW + 1 + loop_blocks)
                sp.dma_start(raw[:, n % RAW, :], dram).then_inc(raw_landed[n % RAW], 16)

            def loads(first, end):
                for n in range(first, end):
                    load(n, weights[DRAM[n]])

            def mlp(layer, half):
                for a, b, what in segments(layer, half):
                    n0 = BLOCK["w1", layer, half, a, 0]
                    if b - a > 1:
                        with sp.Fori(0, b - a) as i:
                            for k in range(CHUNK_BLOCKS):
                                at = i * CHUNK_BLOCKS + (DRAM[n0] + k)
                                load(n0 + k, weights[bass.ds(at, 1), :, :].rearrange("o p f -> (o p) f"),
                                     i * CHUNK_BLOCKS)
                    else:
                        loads(n0, n0 + CHUNK_BLOCKS)

            loads(0, POOL_BLOCKS)
            mlp(0, 0)
            mlp(0, 1)
            loads(BLOCK["gate", 0], BLOCK["w1", 1, 0, 0, 0])
            mlp(1, 0)
            mlp(1, 1)

        @block.tensor
        def _(pe):
            def split_ready(n, add=0):
                pe.wait_ge(hi_ready, n + 1 + add)
                pe.wait_ge(lo_ready, n + 1 + add)

            def bank_free(g, i=0):
                if g >= BANKS:
                    who, count = EVAC[g - BANKS]
                    pe.wait_ge(evac_s[who], count + i * EVACS[who])

            def keep_clock(o, times):
                for _ in range(times):
                    nc.tensor.matmul(o[:, :], ones[:, :], ones_row[:, :], start=True, stop=True)

            def sum_squares(n, tiles=range(KT)):
                for k in tiles:
                    at = KT * FOREGROUND.index(n) + k
                    pe.wait_ge(sq_ready, at + 1)
                    nc.tensor.matmul(core[3][:, :], ones[:, :], squares[k],
                                     start=(k == 0), stop=(k == KT - 1)).then_inc(sq_summed, 1)

            def three_passes(g, slot, cols_of, hi, lo, tiles, before=None):
                n, o = len(tiles), bank[g % BANKS][:, :]
                for k, t in enumerate(tiles):
                    if before:
                        before(k)
                    c = cols_of(k)
                    a, b = w_hi[:, slot, c:c + P], w_lo[:, slot, c:c + P]
                    nc.tensor.matmul(o, a, hi[:, t, :], start=(k == 0), stop=False)
                    nc.tensor.matmul(o, a, lo[:, t, :], start=False, stop=False)
                    last = nc.tensor.matmul(o, b, hi[:, t, :], start=False, stop=(k == n - 1))
                last.then_inc(group_done, 1)

            def window_tile(half, k):
                w, at = k // 2, KT * half + k
                o = core[at % 3]
                if at >= 3:
                    pe.wait_ge(pooled_ready, at - 2)
                for c in range(CPH):
                    i = half * CPH + c
                    pe.wait_ge(bands_ready, i + 1)
                    f = slice(k * P, (k + 1) * P)
                    last = nc.tensor.matmul(o[:, c * LC:(c + 1) * LC], x_tok(half, c)[:, f],
                                            self_band[c][:, w * P:(w + 1) * P],
                                            start=True, stop=(i == 0))
                    if i:
                        last = nc.tensor.matmul(o[:, c * LC:c * LC + HALO], x_tok(half, c - 1)[:, f],
                                                next_band[i - 1][:, w * HALO:(w + 1) * HALO],
                                                start=False, stop=True)
                last.then_inc(windows_done, 1)

            def pool_group(half, d):
                b, w = d // 4, d // 2
                split_ready(BLOCK["pool", b])
                g = GROUPS["pool", half, d]
                bank_free(g)
                pe.wait_ge(pooled_ready, KT * half + 2 * w + 2)
                three_passes(g, BLOCK["pool", b] % SPLIT,
                             lambda k: (2 * (w % 2) + k) * GROUP + (d % 2) * P,
                             hn_hi[half], hn_lo[half], [2 * w, 2 * w + 1])

            def second_product(n0, g0, tile0, i=0):
                split_ready(n0, i * CHUNK_BLOCKS)
                for ks in (range(FT - 1), [FT - 1]):
                    for d in range(2):
                        if ks[0] == 0:
                            bank_free(g0 + d, i)
                        o = bank[(g0 + d) % BANKS][:, :]
                        for k in ks:
                            if d == 0:
                                pe.wait_ge(hid_ready, tile0 + k + 1 + i * FT)
                            c = k * 2 * P + d * P
                            a, b = w_hi[:, n0 % SPLIT, c:c + P], w_lo[:, n0 % SPLIT, c:c + P]
                            nc.tensor.matmul(o, a, hid_hi[:, k, :], start=(k == 0), stop=False)
                            nc.tensor.matmul(o, a, hid_lo[:, k, :], start=False, stop=False)
                            last = nc.tensor.matmul(o, b, hid_hi[:, k, :], start=False, stop=(k == FT - 1))
                        if k == FT - 1:
                            last.then_inc(group_done, 1)
                for b in range(1, W2_BLOCKS):
                    split_ready(n0 + b, i * CHUNK_BLOCKS)
                    for d in range(2):
                        g = g0 + 2 * b + d
                        bank_free(g, i)
                        three_passes(g, (n0 + b) % SPLIT, lambda k: k * 2 * P + d * P, hid_hi, hid_lo, range(FT))

            def mlp(layer, half):
                first_of_all = (layer, half) == (0, 0)
                if not first_of_all:
                    pe.wait_ge(hn_ready, CHAIN["pool" if layer == 0 else "lstm", half] + 1)
                for a, b, what in segments(layer, half):
                    def chunk(i):
                        n0 = BLOCK["w1", layer, half, a, 0]
                        g0 = GROUPS["w1", layer, half, a, 0]
                        for f in range(W1_BLOCKS):
                            split_ready(n0 + f, i * CHUNK_BLOCKS)
                            bank_free(g0 + f, i)
                            follow = first_of_all and a == 0 and f == 0
                            three_passes(g0 + f, (n0 + f) % SPLIT, lambda k: k * P,
                                         hn_hi[half], hn_lo[half], range(KT),
                                         (lambda k: pe.wait_ge(hn0_tiles, k + 1)) if follow else None)
                        second_product(n0 + W1_BLOCKS, g0 + W1_BLOCKS, hid_tile(layer, half, a), i)

                    if b - a > 1:
                        with pe.Fori(0, b - a) as i:
                            chunk(i)
                    else:
                        chunk(0)

            def project(key, n, half):
                split_ready(n)
                bank_free(GROUPS[key])
                three_passes(GROUPS[key], n % SPLIT, lambda k: k * P, hn_hi[half], hn_lo[half], range(KT))

            def turn_gates(half):
                pe.wait_ge(gate_rows, half + 1)
                if half:
                    pe.wait_ge(hnorm_ready, HEADS * half)
                for c in range(CPH):
                    last = nc.tensor.transpose(core[3][:, c * P:(c + 1) * P], rows[:, c * LC:(c + 1) * LC], ident)
                last.then_inc(gate_cols, 1)

            def turn(j):
                pe.wait_ge(qk_ready, 2 * (j + 1))
                evacuated(pe, ("head", j, 2))
                if j:
                    pe.wait_ge(gated_ready, j)
                    pe.wait_ge(state_ready, j)
                    pe.wait_ge(hnorm_ready, j)
                for c in range(CPH):
                    s = slice(c * LC, (c + 1) * LC)
                    nc.tensor.transpose(core[0][:, s], kT[:, s], ident)
                for c in range(CPH):
                    s = slice(c * LC, (c + 1) * LC)
                    nc.tensor.transpose(core[1][:, s], vT[:, s], ident)
                for c in range(CPH):
                    s = slice(c * LC, (c + 1) * LC)
                    last = nc.tensor.matmul(core[2][:, s], kT[:, s], qT[:, j % 2, s], start=True, stop=True)
                last.then_inc(turned, 1)

            W = HEAD_DIM + 1

            def updates(j):
                pe.wait_ge(kw_ready, j + 1)
                pe.wait_ge(vtok_ready, j + 1)
                for c in range(CPH):
                    o = core[c // 2][:, (c % 2) * W:(c % 2 + 1) * W]
                    last = nc.tensor.matmul(o, kw[:, c * LC:(c + 1) * LC], v_tok[:, c, :], start=True, stop=True)
                last.then_inc(update_done, 1)

            def numerators(j):
                pe.wait_ge(prob_ready, j + 1)
                pe.wait_ge(qs_ready, j + 1)
                pe.wait_ge(gate_cols_ready, j // HEADS + 1)
                for c in range(CPH):
                    s = slice(c * LC, (c + 1) * LC)
                    o = core[2 + c // 2][:, (c % 2) * W:(c % 2 + 1) * W]
                    nc.tensor.matmul(o, prob[:, s], v_tok[:, c, :], start=True, stop=False)
                    if c:
                        pe.wait_ge(mid_ready, (CPH - 1) * j + c)
                    last = nc.tensor.matmul(o, qs[:, s], state[:, j % HEADS, :] if c == 0 else mid[:, c - 1, :],
                                            start=False, stop=True)
                last.then_inc(num_done, 1)

            def turn_back(j):
                pe.wait_ge(hnorm_ready, j + 1)
                pe.wait_ge(state_ready, j + 1)
                for c in range(CPH):
                    s = slice(c * LC, (c + 1) * LC)
                    last = nc.tensor.transpose(core[0][:, s], hnorm[:, s], ident)
                last.then_inc(hT_done, 1)

            def lstm():
                pe.wait_ge(vecs_in_s, 32)
                for j in range(STEPS + 1):
                    half = j // HEADS
                    g = heads_out(j)
                    if g is not None:
                        second_product(BLOCK["out", g, 0], GROUPS["out", g, 0], hid_tile("lstm", 0, g))
                    if j < STEPS and j % HEADS == 0:
                        pe.wait_ge(hn_ready, CHAIN["mlp0", half] + 1)
                        project(("gate", half), BLOCK["gate", half], half)
                    for t, work in enumerate((turn, updates, numerators, turn_back)):
                        if j < STEPS:
                            project(("head", j, t), BLOCK["head", j, t], half)
                        if t == 0 and j % HEADS == 1:
                            turn_gates(half)
                        if j:
                            work(j - 1)
                g = STEPS // FT - 1
                second_product(BLOCK["out", g, 0], GROUPS["out", g, 0], hid_tile("lstm", 0, g))

            pe.wait_ge(consts_set, 3)
            keep_clock(core[3], 12)
            for k in range(KT):
                window_tile(0, k)
            for d in range(KT):
                pool_group(0, d)
            pe.wait_ge(x_halo_s, 16)
            for k in range(3):
                window_tile(1, k)
            sum_squares(0)
            evacuated(pe, ("pool", 0, KT - 1))
            keep_clock(bank[3], 9)
            for step in SECOND_POOL:
                k = int(step[1])
                if step[0] == "W":
                    window_tile(1, k)
                elif step[0] == "G":
                    pool_group(1, k)
                else:
                    sum_squares(1, [k])
            mlp(0, 0)
            mlp(0, 1)
            lstm()
            mlp(1, 0)
            mlp(1, 1)
            sum_squares(NORMS - 1)

        def normed(eng, steps, outs, src, gain):
            g = vecs[:, gain:gain + 1]
            if eng is not nc.gpsimd:
                for o in outs:
                    ins = eng.scalar_tensor_tensor(out=o, in0=src, scalar=g, in1=rstd[:, :],
                                                   op0=ALU.mult, op1=ALU.mult)
                return ins
            steps.finish(eng.tensor_tensor(step_t[:, :], src, rstd[:, :], ALU.mult))
            for o in reversed(outs):
                ins = eng.tensor_scalar(o, step_t[:, :], g, 1.0, ALU.mult, ALU.mult)
            return ins

        def sum_of_squares(eng, steps, src, n):
            for k in range(KT):
                if k == 0:
                    steps.finish(eng.tensor_tensor(acc[:, :], src[:, k, :], src[:, k, :], ALU.mult))
                    continue
                steps.finish(eng.tensor_tensor(sq[:, :], src[:, k, :], src[:, k, :], ALU.mult))
                ins = eng.tensor_tensor(acc[:, :], acc[:, :], sq[:, :], ALU.add)
                if k < KT - 1:
                    steps.finish(ins)
            ins.then_inc(acc_ready, 1)

        def by(chain):
            if chain in (0, len(CHAINS) - 1):
                return "act", int(chain > 0)
            return "pool", chain - 1

        def xold_load(eng, chain, k):
            (_, half), _, _, source = CHAINS[chain]
            at = KT * chain + k
            if at >= 2:
                eng.wait_ge(xold_used, at - 1)
            src = x_in[half, k] if source == "input" else x_scratch[half, k]
            eng.dma_start(xold[:, at % 2, :], src).then_inc(xold_landed[by(chain)[0]][at % 2], 16)

        def xnew_store(eng, chain, k):
            (_, half), _, pre, _ = CHAINS[chain]
            eng.wait_ge(xnew_ready, KT * chain + k + 1)
            if pre is None:
                eng.dma_start(out[half, k], y[half][:, k, :]).then_inc(out_stored[by(chain)[0]], 16)
            else:
                eng.dma_start(x_scratch[half, k], y[half][:, k, :]).then_inc(stored[by(chain)[0]], 16)

        def add_residual(eng, steps, chain, dma, beside=None):
            (_, half), post, _, _ = CHAINS[chain]
            eng.wait_ge(rstd_ready, NORM_POST[chain] + 1)
            if dma:
                xold_load(eng, chain, 0)
            for k in range(KT):
                if dma and k + 1 < KT:
                    xold_load(eng, chain, k + 1)
                at = KT * chain + k
                last = chain == len(CHAINS) - 1
                old = y[0][:, k, :] if last else xold[:, at % 2, :]
                scaled = steps.begin(normed(eng, steps, [step_t[:, :]], y[half][:, k, :], post + k))
                if beside:
                    beside(k)
                steps.end(scaled)
                who, before = by(chain)
                if last:
                    eng.wait_ge(x_last_landed, 16)
                else:
                    eng.wait_ge(xold_landed[who][at % 2], 16 * (before * KT // 2 + k // 2 + 1))
                eng.tensor_tensor(y[half][:, k, :], old, step_t[:, :], ALU.add).then_inc(xnew_ready, 1)
                eng.wait_ge(xnew_ready, at + 1)
                eng.sem_inc(xold_used, 1)
                if dma:
                    xnew_store(eng, chain, k)

        def norm_parts(eng, steps, half, gain, n):
            eng.wait_ge(rstd_ready, n + 1)
            for k in range(KT):
                steps.finish(normed(eng, steps, [step_t[:, :], hn_hi[half][:, k, :]], y[half][:, k, :], gain + k))
                steps.finish(eng.tensor_tensor(hn_lo[half][:, k, :], step_t[:, :],
                                               hn_hi[half][:, k, :].bitcast(F32), ALU.subtract))

        def chain_work(eng, steps, chain, dma):
            (_, half), _, pre, _ = CHAINS[chain]
            add_residual(eng, steps, chain, dma)
            if pre is not None:
                sum_of_squares(eng, steps, y[half], NORM_PRE[chain])

        def chain_end(eng, steps, chain):
            (_, half), _, pre, _ = CHAINS[chain]
            norm_parts(eng, steps, half, pre, NORM_PRE[chain])
            who, before = by(chain)
            eng.wait_ge(stored[who], 16 * KT * (before + 1))
            eng.sem_inc(hn_ready, 1)

        @block.gpsimd
        def _(pool):
            steps = OwnSteps(pool, pool_own)

            def total(n):
                pool.wait_ge(acc_ready, n - BACKGROUND + 1)
                pool.wait_ge(rstd_ready, n)
                nc.gpsimd.partition_all_reduce(tot[:, :], acc[:, :], P, RADD).then_inc(tot_ready, 1)

            def background(chain):
                key, _, pre, _ = CHAINS[chain]
                half = key[1]
                evacuated(pool, LAST_GROUP[key])
                sum_of_squares(pool, steps, y[half], NORM_POST[chain])
                total(NORM_POST[chain])
                chain_work(pool, steps, chain, True)
                if pre is not None:
                    total(NORM_PRE[chain])
                    chain_end(pool, steps, chain)

            pool.memset(eps[:, :], EPS).then_inc(consts_set, 1)
            pool.memset(ones[:, :], 1.0).then_inc(consts_set, 1)
            pool.memset(ones_row[:, :], 1.0).then_inc(consts_set, 1)
            pool.wait_ge(vecs_in_s, 32)
            for chain in range(1, len(CHAINS) - 1):
                background(chain)
            pool.wait_ge(out_stored["pool"], 16 * KT)

        @block.scalar
        def _(act):
            steps = OwnSteps(act, act_own)

            def split_hi(n, add=0, landed=0):
                if n >= NB:
                    return
                act.wait_ge(raw_landed[n % RAW], 16 * (n // RAW + 1) + landed)
                if n >= SPLIT:
                    act.wait_ge(group_done, BLOCK_END[n - SPLIT] + add)
                nc.scalar.copy(w_hi[:, n % SPLIT, :], raw[:, n % RAW, :]).then_inc(hi_ready, 1)

            def root(n):
                src = tot
                if n in FOREGROUND:
                    act.wait_ge(sq_summed, KT * (FOREGROUND.index(n) + 1))
                    src = core[3]
                    if n:
                        act.wait_ge(rstd_ready, n)
                else:
                    act.wait_ge(tot_ready, n - BACKGROUND + 1)
                nc.scalar.activation(tot[:, :], src[:, :], ACT.Sqrt, bias=eps[:, :], scale=1.0 / D).then_inc(std_ready, 1)

            def mlp(layer, half):
                for a, b, what in segments(layer, half):
                    n0 = BLOCK["w1", layer, half, a, 0]
                    g0 = GROUPS["w1", layer, half, a, 0]
                    t0 = hid_tile(layer, half, a)

                    def chunk(i):
                        for k in range(CHUNK_BLOCKS):
                            split_hi(n0 + k + 1, i * 12, i * (16 * CHUNK_BLOCKS // RAW))
                            if k >= W1_BLOCKS:
                                continue
                            act.wait_ge(group_done, g0 + k + 1 + i * 12)
                            if t0 + k >= 2:
                                act.wait_ge(hid_ready, t0 + k - 1 + i * FT)
                            r = relu[k % 2][:, :]
                            nc.scalar.activation(r, bank[(g0 + k) % BANKS][:, :], ACT.Relu).then_inc(evac_s["act"], 1)
                            act.wait_ge(evac_s["act"], EVAC[g0 + k][1] + i * EVACS["act"])
                            nc.scalar.activation(hid_hi[:, k, :], r, ACT.Square).then_inc(hidhi_ready, 1)

                    if b - a > 1:
                        with act.Fori(0, b - a) as i:
                            chunk(i)
                    else:
                        chunk(0)
                    if what == "norm":
                        root(norms.pop(0))

            def gates(half):
                t = [y[half][0:HEADS, i, :] for i in range(8)]
                act.wait_ge(gate_z, half + 1)
                steps.finish(nc.scalar.activation(t[2], t[1], ACT.Abs))
                steps.finish(nc.scalar.activation(t[3], t[2], ACT.Exp, scale=-1.0))
                nc.scalar.activation(t[4], t[3], ACT.Ln, bias=1.0).then_inc(gate_l, 1)

            def gate_weights(half):
                t = [y[half][0:HEADS, i, :] for i in range(8)]
                act.wait_ge(gate_args, half + 1)
                if half:
                    act.wait_ge(gate_cols, half)
                nc.scalar.activation(rows[64:64 + HEADS, :], t[5], ACT.Exp)
                nc.scalar.activation(t[6], t[6], ACT.Exp)
                nc.scalar.activation(rows[96:96 + HEADS, :], t[7], ACT.Exp, scale=-1.0).then_inc(gate_exp, 1)
                act.wait_ge(gate_exp, half + 1)
                act.dma_start(row_scratch[half, 0], t[3]).then_inc(rows_stored, 16)
                act.dma_start(row_scratch[half, 1], rows[64:64 + HEADS, :]).then_inc(rows_stored, 16)

            def lstm():
                for j in range(STEPS + 1):
                    half = j // HEADS
                    g = heads_out(j)
                    if j in LSTM_NORM_STEPS:
                        root(norms.pop(0))
                    if g is not None:
                        for b in range(W2_BLOCKS):
                            split_hi(BLOCK["out", g, b] + 1)
                    if j == STEPS:
                        decay_matrix(j - 1)
                        by_tokens(j - 1)
                        head_norm(j - 1)
                        continue
                    if j % HEADS == 0:
                        split_hi(BLOCK["gate", half] + 1)
                    split_hi(BLOCK["head", j, 0] + 1)
                    if j % HEADS == 1:
                        act.wait_ge(rows_stored, 32 * (half + 1))
                        rows_to_all(j - 1)
                    conv_input(j, 0)
                    if j:
                        work = (by_tokens, decay_matrix) if j % HEADS == 1 else (decay_matrix, by_tokens)
                        for f in work:
                            f(j - 1)
                    split_hi(BLOCK["head", j, 1] + 1)
                    if j % HEADS == 0:
                        gates(half)
                    act.wait_ge(conv_ready, 2 * j + 1)
                    if j >= 2:
                        act.wait_ge(qs_ready, j - 1)
                        act.wait_ge(turned, j - 1)
                    nc.scalar.activation(qT[:, j % 2, :], win[:, 0, HALO:], ACT.Silu).then_inc(qk_ready, 1)
                    if j % HEADS:
                        rows_to_all(j)
                    conv_input(j, 1)
                    split_hi(BLOCK["head", j, 2] + 1)
                    act.wait_ge(conv_ready, 2 * j + 2)
                    nc.scalar.activation(kT[:, :], win[:, 1, HALO:], ACT.Silu).then_inc(qk_ready, 1)
                    act.wait_ge(group_done, GROUPS["head", j, 2] + 1)
                    nc.scalar.copy(vT[:, :], bank[GROUPS["head", j, 2] % BANKS][:, :]).then_inc(evac_s["act"], 1)
                    split_hi(BLOCK["head", j, 3] + 1)
                    if j:
                        head_squares(j - 1)
                        head_root(j - 1)
                    act.wait_ge(group_done, GROUPS["head", j, 3] + 1)
                    if j >= 2:
                        act.wait_ge(gated_ready, j - 1)
                    nc.scalar.activation(oT[:, j % 2, :], bank[GROUPS["head", j, 3] % BANKS][:, :],
                                         ACT.Sigmoid).then_inc(evac_s["act"], 1)
                    if j % HEADS == 0:
                        gate_weights(half)
                g = STEPS // FT - 1
                for b in range(W2_BLOCKS):
                    split_hi(BLOCK["out", g, b] + 1)

            def conv_input(j, t):
                act.wait_ge(group_done, GROUPS["head", j, t] + 1)
                if j:
                    act.wait_ge(conv_ready, 2 * j - 1 + t)
                nc.scalar.copy(craw[:, t, HALO:], bank[GROUPS["head", j, t] % BANKS][:, :]).then_inc(evac_s["act"], 1)

            def rows_to_all(j):
                if j >= 2:
                    act.wait_ge(prob_ready, j - 1)
                    act.wait_ge(state_ready, j - 1)
                    act.wait_ge(qs_ready, j - 1)
                for r, dst in enumerate((mx_b, inter_b)):
                    act.dma_start(dst[:, j % 2, :],
                                  row_scratch[j // HEADS, r, j % HEADS:j % HEADS + 1, :].to_broadcast([P, T])
                                  ).then_inc(bcast_landed[j % 2], 16)

            def decay_matrix(j):
                h, head = j // HEADS, j % HEADS
                act.wait_ge(mm_ready, j + 1)
                act.wait_ge(gate_cols_ready, h + 1)
                for c in range(CPH):
                    s = slice(c * LC, (c + 1) * LC)
                    last = nc.scalar.activation(mx_b[:, j % 2, s], mx_b[:, j % 2, s], ACT.Exp,
                                                bias=cols[:, h, c, head:head + 1])
                last.then_inc(decays, 1)

            def by_tokens(j):
                h, head = j // HEADS, j % HEADS
                act.wait_ge(gate_cols_ready, h + 1)
                act.wait_ge(turned, j + 1)
                if j:
                    act.wait_ge(num_done, j)
                for c in range(CPH):
                    s = slice(c * LC, (c + 1) * LC)
                    last = nc.scalar.activation(kw[:, s], core[0][:, s], ACT.Copy,
                                                scale=cols[:, h, c, 32 + head:33 + head])
                last.then_inc(kw_ready, 1)
                nc.scalar.copy(v_tok[:, :, 0:HEAD_DIM],
                               core[1][:, :].rearrange("p (c d) -> p c d", c=CPH)).then_inc(vtok_ready, 1)

            def head_squares(j):
                act.wait_ge(num_done, j + 1)
                if j:
                    act.wait_ge(hT_done, j)
                for c in range(CPH):
                    o = (c % 2) * (HEAD_DIM + 1)
                    last = nc.scalar.activation(hnorm[:, c * LC:(c + 1) * LC],
                                                core[2 + c // 2][:, o:o + HEAD_DIM], ACT.Square,
                                                accum_out=small[:, 0, c:c + 1])
                last.then_inc(ssq_ready, 1)

            def head_root(j):
                act.wait_ge(den_ready, j + 1)
                nc.scalar.activation(small[:, 6, :], small[:, 5, :], ACT.Sqrt, bias=eps[:, :],
                                     scale=1.0 / HEAD_DIM).then_inc(hstd_ready, 1)

            def head_norm(j):
                head_squares(j)
                head_root(j)

            def square(n, k):
                i = FOREGROUND.index(n)
                half = 1 if n == NORMS - 1 else 0
                if i:
                    act.wait_ge(sq_summed, KT * (i - 1) + k + 1)
                nc.scalar.activation(squares[k], y[half][:, k, :], ACT.Square).then_inc(sq_ready, 1)

            def token_roots(half):
                for c in range(half * CPH, (half + 1) * CPH):
                    act.wait_ge(x_tok_s[c], 16)
                    steps.finish(nc.scalar.activation(token_sq, x_tok(half, c % CPH), ACT.Square,
                                                      accum_out=ssq[:, 0, c:c + 1]))
                s = slice(half * CPH, (half + 1) * CPH)
                act.wait_ge(consts_set, 1)
                nc.scalar.activation(ssq[:, 1, s], ssq[:, 0, s], ACT.Sqrt, bias=eps[:, :],
                                     scale=1.0 / D).then_inc(tok_std, 1)

            def pooled_high(half, k):
                at = KT * half + k
                act.wait_ge(windows_done, at + 1)
                nc.scalar.activation(hn_hi[half][:, k, :], core[at % 3][:, :], ACT.Copy,
                                     scale=vecs[:, V_MIX_PRE + k:V_MIX_PRE + k + 1]).then_inc(pooled_hi, 1)

            def pool_out(half, k):
                g = GROUPS["pool", half, k]
                act.wait_ge(group_done, g + 1)
                nc.scalar.activation(y[half][:, k, :], bank[g % BANKS][:, :], ACT.Identity,
                                     bias=pool_bs[:, k:k + 1],
                                     scale=vecs[:, V_POOL_S + k:V_POOL_S + k + 1]).then_inc(evac_s["act"], 1)

            norms = list(range(NORMS))
            for c in range(CPH):
                act.dma_start(x_tok(0, c), x_tokens[0, c]).then_inc(x_tok_s[c], 16)
            act.dma_start(consts[:, :], consts_in).then_inc(vecs_in_s, 16)
            act.dma_start(vecs[:, :], vecs_in).then_inc(vecs_in_s, 16)
            act.dma_start(band_consts, bands_in).then_inc(bands_in_s, 16)
            for c in range(CPH):
                act.dma_start(x_tok(1, c), x_tokens[1, c]).then_inc(x_tok_s[CPH + c], 16)
            act.dma_start(x_halo, x_tokens[0, CPH - 1]).then_inc(x_halo_s, 16)
            token_roots(0)
            for b in range(POOL_BLOCKS):
                split_hi(b)
            act.wait_ge(vecs_in_s, 32)
            for k in range(KT):
                pooled_high(0, k)
            token_roots(1)
            act.wait_ge(bs_ready, 1)
            for k in range(KT):
                pool_out(0, k)
                act.wait_ge(evac_s["act"], EVAC[GROUPS["pool", 0, k]][1])
                square(0, k)
            for k in range(2):
                xold_load(act, 0, k)
            root(norms.pop(0))
            for k in range(KT):
                pooled_high(1, k)
                xnew_store(act, 0, k)
                square(1, k)
                if k + 2 < KT:
                    xold_load(act, 0, k + 2)
                if k >= 6:
                    for d in range(2):
                        pool_out(1, 2 * (k - 6) + d)
            split_hi(POOL_BLOCKS)
            root(norms.pop(0))
            for d in range(4, KT):
                pool_out(1, d)
            for k in range(KT):
                act.wait_ge(hn0_part, k + 1)
                nc.scalar.copy(hn_hi[0][:, k, :], parts[k % 2]).then_inc(hn0_hi, 1)
            mlp(0, 0)
            mlp(0, 1)
            lstm()
            mlp(1, 0)
            mlp(1, 1)
            last = len(CHAINS) - 1
            act.wait_ge(out_stored["pool"], 16 * KT)
            act.dma_start(y[0][:, :, :], x_scratch[1].rearrange("k p t -> p k t")).then_inc(x_last_landed, 16)
            for k in range(KT):
                evacuated(act, ("w2", 1, 1, CHUNKS - 1, k))
                square(NORMS - 1, k)
            root(norms.pop(0))
            for k in range(KT):
                xnew_store(act, last, k)
            act.wait_ge(out_stored["act"], 16 * KT)

        @block.vector
        def _(dve):
            steps = OwnSteps(dve, dve_own)
            norms = list(range(NORMS))

            def split_lo(n, add_b=0, add_g=0):
                if n >= NB:
                    return
                dve.wait_ge(hi_ready, n + 1 + add_b)
                dve.tensor_tensor(w_lo[:, n % SPLIT, :], raw[:, n % RAW, :],
                                  w_hi[:, n % SPLIT, :].bitcast(F32), ALU.subtract).then_inc(lo_ready, 1)

            def reciprocal_root(n):
                dve.wait_ge(std_ready, n + 1)
                dve.reciprocal(rstd[:, :], tot[:, :]).then_inc(rstd_ready, 1)

            def token_bands(half):
                dve.wait_ge(tok_std, half + 1)
                dve.wait_ge(bands_in_s, 16)
                s = slice(half * CPH, (half + 1) * CPH)
                steps.finish(dve.reciprocal(rs[:, s], ssq[:, 1, s]))
                if half:
                    dve.wait_ge(windows_done, KT)
                for c in range(CPH):
                    i = half * CPH + c
                    r = rs[:, i:i + 1]
                    dve.tensor_scalar(next_band[i], band_consts[:, B_NEXT:B_FIRST], r, None, ALU.mult)
                    ins = dve.tensor_scalar(self_band[c], band_consts[:, B_SELF:B_NEXT], r, None, ALU.mult)
                    if i == 0:
                        steps.finish(ins)
                        ins = dve.tensor_scalar(
                            self_band[c].rearrange("p (w n) -> p w n", w=NW)[:, :, 0:HALO],
                            band_consts[:, B_FIRST:BANDS].rearrange("p (w n) -> p w n", w=NW),
                            r, None, ALU.mult)
                    ins.then_inc(bands_ready, 1)

            def pooled_low(half, k):
                at = KT * half + k
                dve.wait_ge(pooled_hi, at + 1)
                dve.scalar_tensor_tensor(out=hn_lo[half][:, k, :], in0=core[at % 3][:, :],
                                         scalar=vecs[:, V_MIX_PRE + k:V_MIX_PRE + k + 1],
                                         in1=hn_hi[half][:, k, :].bitcast(F32),
                                         op0=ALU.mult, op1=ALU.subtract).then_inc(pooled_ready, 1)

            def take_out(half, n0, g0, first, add_b=0, add_g=0):
                for b in range(W2_BLOCKS):
                    split_lo(n0 + b + 1, add_b)
                    for d in range(2):
                        k = 2 * b + d
                        g = g0 + k
                        dve.wait_ge(group_done, g + 1 + add_g)
                        if first:
                            dve.tensor_copy(y[half][:, k, :], bank[g % BANKS][:, :]).then_inc(evac_s["dve"], 1)
                        else:
                            dve.tensor_tensor(y[half][:, k, :], bank[g % BANKS][:, :], y[half][:, k, :],
                                              ALU.add).then_inc(evac_s["dve"], 1)

            def mlp(layer, half):
                for a, b, what in segments(layer, half):
                    n0 = BLOCK["w1", layer, half, a, 0]
                    g0 = GROUPS["w1", layer, half, a, 0]

                    t0 = hid_tile(layer, half, a)
                    m0 = (2 * layer + half) * CHUNKS * FT + a * FT

                    def chunk(i):
                        for f in range(W1_BLOCKS):
                            split_lo(n0 + f + 1, i * CHUNK_BLOCKS)
                            dve.wait_ge(evac_s["act"], EVAC[g0 + f][1] + i * EVACS["act"])
                            r = relu[f % 2][:, :]
                            if t0 + f:
                                dve.wait_ge(hid_ready, t0 + f + i * FT)
                            steps.finish(dve.tensor_tensor(relu_sq[:, :], r, r, ALU.mult))
                            dve.wait_ge(hidhi_ready, m0 + f + 1 + i * FT)
                            dve.tensor_tensor(hid_lo[:, f, :], relu_sq[:, :], hid_hi[:, f, :].bitcast(F32),
                                              ALU.subtract).then_inc(hid_ready, 1)
                        take_out(half, n0 + W1_BLOCKS, g0 + W1_BLOCKS, a == 0, i * CHUNK_BLOCKS, i * 12)

                    if b - a > 1:
                        with dve.Fori(0, b - a) as i:
                            steps.repeat(i, W1_BLOCKS)
                            chunk(i)
                        steps.repeated(b - a)
                    else:
                        chunk(0)
                    if what == "norm":
                        reciprocal_root(norms.pop(0))

            def gates(half):
                t = [y[half][0:HEADS, i, :] for i in range(8)]
                g = GROUPS["gate", half]
                dve.wait_ge(group_done, g + 1)
                o = bank[g % BANKS]
                bi = V_GATE_B
                fr = GATE_ROW_F
                dve.tensor_scalar(t[1], o[fr:fr + HEADS, :], vecs[fr:fr + HEADS, bi:bi + 1], None,
                                  ALU.add).then_inc(gate_z, 1)
                steps.finish(dve.tensor_scalar(t[0], o[0:HEADS, :], vecs[0:HEADS, bi:bi + 1], None, ALU.add))
                dve.wait_ge(gate_z, half + 1)
                dve.sem_inc(evac_s["dve"], 1)

            def gate_chain(half):
                t = [y[half][0:HEADS, i, :] for i in range(8)]
                dve.wait_ge(gate_l, half + 1)
                steps.finish(dve.scalar_tensor_tensor(out=t[4], in0=t[1], scalar=0.0, in1=t[4],
                                                      op0=ALU.min, op1=ALU.subtract))
                for c in range(CPH):
                    s = slice(c * LC, (c + 1) * LC)
                    ins = dve.tensor_tensor_scan(t[2][:, s], zrow[:, :], t[4][:, s], 0.0, ALU.add, ALU.add)
                steps.finish(ins)
                steps.finish(dve.tensor_tensor(t[0], t[0], t[2], ALU.subtract))
                for c in range(CPH):
                    s = slice(c * LC, (c + 1) * LC)
                    e = (c + 1) * LC
                    i = half * CPH + c
                    steps.finish(dve.tensor_tensor_scan(t[3][:, s], zrow[:, :], t[0][:, s], m_run[:, i:i + 1],
                                                        ALU.add, ALU.max))
                    steps.finish(dve.tensor_tensor(m_run[:, i + 1:i + 2], t[3][:, e - 1:e], t[2][:, e - 1:e], ALU.add))
                    dve.tensor_scalar(t[5][:, s], t[3][:, s], -1.0, m_run[:, i:i + 1], ALU.mult, ALU.add)
                    ins = dve.tensor_scalar(t[6][:, s], t[0][:, s], t[3][:, e - 1:e], None, ALU.subtract)
                steps.finish(ins)
                dve.tensor_tensor(t[7], t[2], t[3], ALU.add).then_inc(gate_args, 1)

            def gate_tail(half):
                t = [y[half][0:HEADS, i, :] for i in range(8)]
                dve.wait_ge(gate_exp, half + 1)
                dve.tensor_copy(rows[0:HEADS, :], t[0])
                steps.finish(dve.tensor_scalar(rows[32:32 + HEADS, :], t[6], KSCALE, None, ALU.mult))
                dve.sem_inc(gate_rows, 1)

            def gate_columns(half):
                dve.wait_ge(gate_cols, half + 1)
                dve.tensor_copy(cols[:, half, :, :].rearrange("p c r -> p (c r)"), core[3][:, :]).then_inc(gate_cols_ready, 1)

            def conv(j, t):
                tile = t * HEADS + j % HEADS
                src = craw[:, t, :]
                dve.wait_ge(evac_s["act"], EVAC[GROUPS["head", j, t]][1])
                steps.finish(dve.tensor_copy(src[:, 0:HALO], taps[:, tile, :]))
                dve.tensor_copy(taps[:, tile, :], src[:, T:T + HALO])
                if j:
                    dve.wait_ge(qk_ready, 2 * j - 1 + t)
                dst = win[:, t, HALO:]
                for i in range(TAPS):
                    lag = TAPS - 1 - i
                    w = vecs[:, V_CONV_W + i * 2 * HEADS + tile:V_CONV_W + i * 2 * HEADS + tile + 1]
                    view = src[:, HALO - lag:HALO + T - lag]
                    if i == 0:
                        steps.finish(dve.tensor_scalar(dst, view, w, vecs[:, V_CONV_B + tile:V_CONV_B + tile + 1],
                                                       ALU.mult, ALU.add))
                    elif i < TAPS - 1:
                        steps.finish(dve.scalar_tensor_tensor(out=dst, in0=view, scalar=w, in1=dst,
                                                              op0=ALU.mult, op1=ALU.add))
                    else:
                        dve.scalar_tensor_tensor(out=dst, in0=view, scalar=w, in1=dst,
                                                 op0=ALU.mult, op1=ALU.add).then_inc(conv_ready, 1)

            def probabilities(j):
                dve.wait_ge(turned, j + 1)
                dve.wait_ge(decays, j + 1)
                if j:
                    dve.wait_ge(num_done, j)
                dve.scalar_tensor_tensor(out=prob[:, :], in0=core[2][:, :], scalar=KSCALE, in1=mx_b[:, j % 2, :],
                                         op0=ALU.mult, op1=ALU.mult).then_inc(prob_ready, 1)

            def states(j):
                dve.wait_ge(update_done, j + 1)
                if j:
                    dve.wait_ge(num_done, j)
                for c in range(CPH - 1):
                    state_after(j, c).then_inc(mid_ready, 1)
                    dve.wait_ge(mid_ready, (CPH - 1) * j + c + 1)

            def state_after(j, c):
                o = core[c // 2][:, (c % 2) * (HEAD_DIM + 1):(c % 2 + 1) * (HEAD_DIM + 1)]
                e = (c + 1) * LC
                before = state[:, j % HEADS, :] if c == 0 else mid[:, c - 1, :]
                after = mid[:, c, :] if c < CPH - 1 else state[:, j % HEADS, :]
                return dve.scalar_tensor_tensor(out=after, in0=before, scalar=inter_b[:, j % 2, e - 1:e], in1=o,
                                                op0=ALU.mult, op1=ALU.add)

            def normalize(j, between):
                h, head = j // HEADS, j % HEADS
                dve.wait_ge(num_done, j + 1)
                state_after(j, CPH - 1).then_inc(state_ready, 1)
                dve.wait_ge(ssq_ready, j + 1)
                for b in range(2):
                    den = core[2 + b][:, 0:2 * (HEAD_DIM + 1)].rearrange("p (c w) -> p c w", c=2)[:, :, HEAD_DIM:HEAD_DIM + 1]
                    ins = dve.tensor_copy(small[:, 1, 2 * b:2 * b + 2].rearrange("p (c o) -> p c o", o=1), den)
                steps.finish(ins)
                steps.finish(dve.scalar_tensor_tensor(out=small[:, 2, :], in0=small[:, 1, :], scalar=-1.0,
                                                      in1=small[:, 1, :], op0=ALU.mult, op1=ALU.max))
                steps.finish(dve.tensor_tensor(small[:, 3, :], small[:, 2, :], cols[:, h, :, 96 + head], ALU.max))
                steps.finish(dve.reciprocal(small[:, 4, :], small[:, 3, :]))
                steps.finish(dve.tensor_tensor(small[:, 1, :], small[:, 0, :], small[:, 4, :], ALU.mult))
                dve.tensor_tensor(small[:, 5, :], small[:, 1, :], small[:, 4, :], ALU.mult).then_inc(den_ready, 1)
                between()
                dve.wait_ge(hstd_ready, j + 1)
                steps.finish(dve.reciprocal(small[:, 7, :], small[:, 6, :]))
                steps.finish(dve.tensor_tensor(small[:, 7, :], small[:, 7, :], small[:, 4, :], ALU.mult))
                for c in range(CPH):
                    o = (c % 2) * (HEAD_DIM + 1)
                    ins = dve.tensor_scalar(hnorm[:, c * LC:(c + 1) * LC], core[2 + c // 2][:, o:o + HEAD_DIM],
                                            small[:, 7, c:c + 1], None, ALU.mult)
                ins.then_inc(hnorm_ready, 1)

            def gate_head(j):
                k = j % HEADS
                dve.wait_ge(hT_done, j + 1)
                dve.wait_ge(evac_s["act"], EVAC[GROUPS["head", j, 3]][1])
                steps.finish(dve.scalar_tensor_tensor(out=relu_sq[:, :], in0=core[0][:, :],
                                                      scalar=vecs[:, V_HEAD_NORM + k:V_HEAD_NORM + k + 1],
                                                      in1=oT[:, j % 2, :], op0=ALU.mult, op1=ALU.mult))
                dve.sem_inc(gated_ready, 1)
                steps.finish(dve.tensor_copy(hid_hi[:, j % FT, :], relu_sq[:, :]))
                dve.tensor_tensor(hid_lo[:, j % FT, :], relu_sq[:, :], hid_hi[:, j % FT, :].bitcast(F32),
                                  ALU.subtract).then_inc(hid_ready, 1)

            def rows_for(j):
                dve.wait_ge(bcast_landed[j % 2], 32 * (j // 2 + 1))
                dve.tensor_tensor(mx_b[:, j % 2, :], mask, mx_b[:, j % 2, :], ALU.subtract).then_inc(mm_ready, 1)
                dve.wait_ge(qk_ready, 2 * j + 1)
                if j:
                    dve.wait_ge(num_done, j)
                dve.tensor_tensor(qs[:, :], qT[:, j % 2, :], inter_b[:, j % 2, :], ALU.mult).then_inc(qs_ready, 1)

            def lstm():
                steps.finish(dve.memset(taps[:, :, :], 0.0))
                for j in range(STEPS + 1):
                    half = j // HEADS
                    g = heads_out(j)
                    if j in LSTM_NORM_STEPS:
                        reciprocal_root(norms.pop(0))
                    if g is not None:
                        take_out(g // 2, BLOCK["out", g, 0], GROUPS["out", g, 0], g % 2 == 0)
                    if j == STEPS:
                        probabilities(j - 1)
                        states(j - 1)
                        normalize(j - 1, lambda: None)
                        gate_head(j - 1)
                        continue
                    if j % HEADS == 0:
                        split_lo(BLOCK["gate", half] + 1)
                        gates(half)
                    split_lo(BLOCK["head", j, 0] + 1)
                    conv(j, 0)
                    if j % HEADS == 1:
                        gate_columns(half)
                        rows_for(j - 1)
                    if j:
                        probabilities(j - 1)
                    split_lo(BLOCK["head", j, 1] + 1)
                    if j % HEADS == 0:
                        gate_chain(half)
                    if j:
                        states(j - 1)
                    if j % HEADS == 0:
                        split_lo(BLOCK["head", j, 2] + 1)
                    conv(j, 1)
                    if j % HEADS:
                        split_lo(BLOCK["head", j, 2] + 1)
                    if j % HEADS:
                        rows_for(j)
                    if j:
                        normalize(j - 1, lambda: split_lo(BLOCK["head", j, 3] + 1))
                        gate_head(j - 1)
                    else:
                        split_lo(BLOCK["head", j, 3] + 1)
                    if j % HEADS == 0:
                        gate_tail(half)
                g = STEPS // FT - 1
                take_out(g // 2, BLOCK["out", g, 0], GROUPS["out", g, 0], g % 2 == 0)

            dve.memset(state[:, :, :], 0.0)
            dve.memset(rows[:, :], 0.0)
            dve.memset(zrow[:, :], 0.0)
            dve.memset(m_run[:, 0:1], 0.0)
            steps.finish(dve.memset(v_tok[:, :, HEAD_DIM:], 1.0))
            dve.wait_ge(vecs_in_s, 32)
            dve.tensor_tensor(pool_bs[:, :], vecs[:, V_POOL_B:V_POOL_B + KT], vecs[:, V_POOL_S:V_POOL_S + KT],
                              ALU.mult).then_inc(bs_ready, 1)
            token_bands(0)
            for b in range(POOL_BLOCKS):
                split_lo(b)
            for k in range(KT):
                pooled_low(0, k)
            token_bands(1)
            reciprocal_root(norms.pop(0))
            add_residual(dve, steps, 0, False, lambda k: pooled_low(1, k))
            split_lo(POOL_BLOCKS)
            reciprocal_root(norms.pop(0))
            dve.wait_ge(rstd_ready, 2)
            for k in range(KT + 1):
                if k < KT:
                    normed(dve, steps, [parts[k % 2]], y[0][:, k, :], V_FFN_PRE + k).then_inc(hn0_part, 1)
                if k:
                    dve.wait_ge(hn0_hi, k)
                    dve.wait_ge(hn0_part, k)
                    dve.tensor_tensor(hn_lo[0][:, k - 1, :], parts[(k - 1) % 2],
                                      hn_hi[0][:, k - 1, :].bitcast(F32), ALU.subtract).then_inc(hn0_tiles, 1)
                    dve.wait_ge(hn0_tiles, k)
            who, before = by(0)
            dve.wait_ge(stored[who], 16 * KT)
            dve.sem_inc(hn_ready, 1)
            mlp(0, 0)
            mlp(0, 1)
            lstm()
            mlp(1, 0)
            mlp(1, 1)
            last = len(CHAINS) - 1
            reciprocal_root(norms.pop(0))
            add_residual(dve, steps, last, False)


def kernel(x, mix_pre_g, mix_post_g, ffn_pre_g, ffn_post_g, pool_w, pool_b, pool_scale,
           mlstm_w_in, mlstm_conv_w, mlstm_conv_b, mlstm_i_bias, mlstm_f_bias,
           mlstm_head_norm_w, mlstm_w_out, mlp_w1, mlp_w2):
    import concourse.bacc as bacc
    from concourse.bass_utils import run_bass_kernel_spmd

    def tiles_of(w, rows, columns):
        n = w.shape[1] // columns
        return w.reshape(rows, P, n, columns).transpose(2, 1, 0, 3).reshape(n, P, rows * columns)

    def mlp_blocks(w1, w2):
        first = tiles_of(w1, KT, P)
        out = []
        for c in range(CHUNKS):
            out.append(first[c * FT:(c + 1) * FT])
            out.append(tiles_of(w2[c * FT * P:(c + 1) * FT * P], FT, 2 * P))
        return out

    x, pool_w, w_in, w_out = (np.asarray(a) for a in (x, pool_w, mlstm_w_in, mlstm_w_out))
    w1, w2 = np.asarray(mlp_w1), np.asarray(mlp_w2)
    pool_blocks = pool_w[0].reshape(2, 2, 2, P, GROUP).transpose(0, 3, 1, 2, 4).reshape(2, P, BLK)
    gate_block = np.zeros((P, KT, P), np.float32)
    gates = w_in[0][:, 4 * D:].reshape(KT, P, 2 * HEADS).transpose(1, 0, 2)
    gate_block[:, :, 0:HEADS] = gates[:, :, 0:HEADS]
    gate_block[:, :, GATE_ROW_F:GATE_ROW_F + HEADS] = gates[:, :, HEADS:]
    heads = tiles_of(w_in[0][:, :4 * D], KT, P).reshape(HEAD_BLOCKS, HEADS, P, BLK).transpose(1, 0, 2, 3)
    outs = [tiles_of(w_out[0][g * FT * P:(g + 1) * FT * P], FT, 2 * P) for g in range(2)]
    stream = np.concatenate([pool_blocks, *mlp_blocks(w1[0], w2[0]), gate_block.reshape(1, P, BLK),
                             heads.reshape(-1, P, BLK), *outs, *mlp_blocks(w1[1], w2[1])])
    assert stream.shape == (DRAM_BLOCKS, P, BLK)

    columns = [np.asarray(a).reshape(-1, P).T for a in (
        mix_pre_g, mix_post_g, ffn_pre_g, ffn_post_g, pool_b, pool_scale, mlstm_conv_w, mlstm_conv_b,
        mlstm_head_norm_w)]
    biases = np.zeros((P, 1), np.float32)
    biases[0:HEADS, 0] = np.asarray(mlstm_i_bias)[0]
    biases[GATE_ROW_F:GATE_ROW_F + HEADS, 0] = np.asarray(mlstm_f_bias)[0]
    vectors = np.ascontiguousarray(np.concatenate([*columns, biases], axis=1))
    assert vectors.shape == (P, VECS)

    at = np.arange(P)
    causal = np.where(at[:, None] <= at[None, :], 0.0, NEG).astype(np.float32)

    def band(w, to, first=False):
        lag = to[None, :] - at[:, None]
        mean = np.where((lag >= 0) & (lag < w), 1.0, 0.0) / (np.minimum(to + 1, w) if first else w)
        return mean - (lag == 0)

    bands = np.concatenate([*[band(w, at) for w in WINDOWS], *[band(w, P + at[:HALO]) for w in WINDOWS],
                            *[band(w, at[:HALO], True) for w in WINDOWS]], axis=1).astype(np.float32)
    constants = np.concatenate([np.eye(P, dtype=np.float32), *[causal] * CPH], axis=1)
    assert constants.shape == (P, CONSTS) and bands.shape == (P, BANDS)

    x_tiles = np.ascontiguousarray(x[0].T.reshape(KT, P, HALVES, T).transpose(2, 0, 1, 3))
    x_tokens = np.ascontiguousarray(x[0].reshape(HALVES, CPH, P, D))
    arrays = {"x_tiles": x_tiles, "x_tokens": x_tokens, "weights": np.ascontiguousarray(stream), "vectors": vectors,
              "constants": np.ascontiguousarray(constants), "bands": bands}

    nc = bacc.Bacc("TRN2", target_bir_lowering=False, num_devices=1)
    args = [nc.dram_tensor(name, a.shape, F32, kind="ExternalInput").ap() for name, a in arrays.items()]
    out = nc.dram_tensor("out_tiles", x_tiles.shape, F32, kind="ExternalOutput").ap()
    build(nc, *args, out)
    result = run_bass_kernel_spmd(nc, [arrays], core_ids=[0]).results[0]["out_tiles"]
    return result.transpose(1, 2, 0, 3).reshape(1, D, SEQ).transpose(0, 2, 1)
```
